# Optimizing a Trainium2 kernel written in Bass

```python
import math
import jax, jax.numpy as jnp
from jax import lax
import numpy as np

D_MODEL = 2048
BATCH = 1
SEQ = 512
DEPTH = 2
DEC_BATCH = 8
DEC_SEQ = 16
PAST_LEN = 128

CHUNK = 64
N_A_LAYERS = DEPTH // 2
N_B_LAYERS = DEPTH - N_A_LAYERS
MIX_WIDTH = (3 * D_MODEL) // 4
MEM_WIDTH = D_MODEL // 4
MEM_HEADS = 4
MEM_HEAD_DIM = MEM_WIDTH // MEM_HEADS
N_MEM = 256
SSM_GROUP = 16
SSM_GROUPS = MIX_WIDTH // SSM_GROUP
SSM_STATE = 64
SB_HEAD_DIM = 128
SB_HEADS = MIX_WIDTH // SB_HEAD_DIM
SB_BLOCK = 128
IN_WIDTH = 2 * MIX_WIDTH + 2 * MEM_WIDTH
OUT_WIDTH = MIX_WIDTH + MEM_WIDTH
EPS = 1e-6
DT_MIN = 1e-3
DT_MAX = 1e-1

kernel_name = 'yoco_s5_stickbreaking_stream_step'

def rms_norm(x, g):
    x32 = x.astype(jnp.float32)
    y = x32 * lax.rsqrt(jnp.mean(x32 * x32, axis=-1, keepdims=True) + EPS) * g.astype(jnp.float32)
    return y.astype(x.dtype)

def mem_attention(q, mk, mv):
    bsz, l = q.shape[:2]
    s = jnp.einsum('bqhd,bmhd->bhqm', q, mk.astype(q.dtype)).astype(jnp.float32) * (1.0 / math.sqrt(MEM_HEAD_DIM))
    p = jax.nn.softmax(s, axis=-1)
    o = jnp.einsum('bhqm,bmhd->bqhd', p.astype(q.dtype), mv.astype(q.dtype))
    return o.reshape(bsz, l, MEM_WIDTH)

def _ssm_combine(e1, e2):
    a1, b1 = e1
    a2, b2 = e2
    return a1 * a2, a2 * b1 + b2

def s5_scan(u, h0, lam_re, lam_im, log_dt, b_re, b_im, c_re, c_im, d):
    f32 = jnp.float32
    lam = lax.complex(lam_re.astype(f32), lam_im.astype(f32))
    dt = jnp.exp(log_dt.astype(f32))[:, None]
    lam_dt = lam * dt
    a_bar = jnp.exp(lam_dt)
    bmat = lax.complex(b_re.astype(f32), b_im.astype(f32))
    b_bar = ((a_bar - 1.0) / lam)[..., None] * bmat
    cmat = lax.complex(c_re.astype(f32), c_im.astype(f32))
    d32 = d.astype(f32)
    bsz, l, g, h = u.shape
    t = CHUNK if l % CHUNK == 0 else l
    n = l // t
    pows = jnp.exp(lam_dt[None] * jnp.arange(1, t + 1, dtype=f32)[:, None, None])
    u_blocks = u.astype(f32).reshape(bsz, n, t, g, h).swapaxes(0, 1)

    def step(h_prev, u_blk):
        bu = jnp.einsum('gph,btgh->btgp', b_bar, u_blk.astype(jnp.complex64))
        a = jnp.broadcast_to(a_bar, bu.shape)
        _, h_loc = lax.associative_scan(_ssm_combine, (a, bu), axis=1)
        hs = h_loc + pows[None] * h_prev[:, None]
        y = jnp.real(jnp.einsum('ghp,btgp->btgh', cmat, hs)) + d32 * u_blk
        return hs[:, -1], y

    h_last, y = lax.scan(step, h0, u_blocks)
    y = y.swapaxes(0, 1).reshape(bsz, l, g, h)
    return y, h_last

def stick_breaking_attention(q, k, v, q_offset):
    bsz, lq, nh, hd = q.shape
    lk = k.shape[1]
    blk = SB_BLOCK if lq % SB_BLOCK == 0 else lq
    nblk = lq // blk
    scale = 1.0 / math.sqrt(hd)
    k_pos = jnp.arange(lk)
    q_blocks = q.reshape(bsz, nblk, blk, nh, hd).swapaxes(0, 1)
    k = k.astype(q.dtype)
    v = v.astype(q.dtype)

    def one_block(args):
        q_blk, b_idx = args
        q_pos = q_offset + b_idx * blk + jnp.arange(blk)
        z = jnp.einsum('bqhd,bkhd->bhqk', q_blk, k).astype(jnp.float32) * scale
        causal = k_pos[None, :] < q_pos[:, None]
        log_keep = jnp.where(causal, jax.nn.log_sigmoid(-z), 0.0)
        later = lax.cumsum(log_keep, axis=3, reverse=True) - log_keep
        w = jnp.where(causal, jnp.exp(jax.nn.log_sigmoid(z) + later), 0.0)
        return jnp.einsum('bhqk,bkhd->bqhd', w.astype(v.dtype), v)

    out = lax.map(one_block, (q_blocks, jnp.arange(nblk)))
    return out.swapaxes(0, 1).reshape(bsz, lq, nh, hd)

def _split_proj(proj):
    return jnp.split(proj, [MIX_WIDTH, 2 * MIX_WIDTH, 2 * MIX_WIDTH + MEM_WIDTH], axis=-1)

def layer_a(x, h0, mk, mv, w_in, w_out, g_pre, g_post, lam_re, lam_im, log_dt,
            b_re, b_im, c_re, c_im, d, w_glu, b_glu):
    bsz, l, _ = x.shape
    hn = rms_norm(x, g_pre)
    u, gate, mq, mg = _split_proj(hn @ w_in)
    y, h_last = s5_scan(u.reshape(bsz, l, SSM_GROUPS, SSM_GROUP), h0, lam_re, lam_im, log_dt,
                        b_re, b_im, c_re, c_im, d)
    y = jax.nn.gelu(y.reshape(bsz, l, MIX_WIDTH).astype(x.dtype))
    y = y * jax.nn.sigmoid(y @ w_glu + b_glu)
    a_out = y * jax.nn.silu(gate)
    m_out = mem_attention(mq.reshape(bsz, l, MEM_HEADS, MEM_HEAD_DIM), mk, mv) * jax.nn.silu(mg)
    out = jnp.concatenate([a_out, m_out], axis=-1) @ w_out
    return x + rms_norm(out, g_post), h_last

def layer_b(x, k_all, v_all, q_offset, mk, mv, w_in, w_out, g_pre, g_post):
    bsz, l, _ = x.shape
    hn = rms_norm(x, g_pre)
    q, gate, mq, mg = _split_proj(hn @ w_in)
    o = stick_breaking_attention(q.reshape(bsz, l, SB_HEADS, SB_HEAD_DIM), k_all, v_all, q_offset)
    b_out = o.reshape(bsz, l, MIX_WIDTH) * jax.nn.silu(gate)
    m_out = mem_attention(mq.reshape(bsz, l, MEM_HEADS, MEM_HEAD_DIM), mk, mv) * jax.nn.silu(mg)
    out = jnp.concatenate([b_out, m_out], axis=-1) @ w_out
    return x + rms_norm(out, g_post)

def shared_kv(x, g_kv, w_kv):
    bsz, l, _ = x.shape
    kv = rms_norm(x, g_kv) @ w_kv
    k, v = jnp.split(kv, 2, axis=-1)
    return (k.reshape(bsz, l, SB_HEADS, SB_HEAD_DIM), v.reshape(bsz, l, SB_HEADS, SB_HEAD_DIM))

def trunk(x, mem_k, mem_v, ssm_h0, past_k, past_v, q_offset, p):
    new_h = []
    k_new = v_new = k_all = v_all = None
    for layer in range(DEPTH):
        if layer == N_A_LAYERS:
            k_new, v_new = shared_kv(x, p['g_kv'], p['w_kv'])
            if past_k is None:
                k_all, v_all = k_new, v_new
            else:
                k_all = jnp.concatenate([past_k.astype(k_new.dtype), k_new], axis=1)
                v_all = jnp.concatenate([past_v.astype(v_new.dtype), v_new], axis=1)
        if layer < N_A_LAYERS:
            i = layer
            x, h_last = layer_a(x, ssm_h0[i], mem_k[layer], mem_v[layer], p['w_in_a'][i], p['w_out_a'][i],
                                p['g_pre_a'][i], p['g_post_a'][i], p['ssm_lam_re'][i], p['ssm_lam_im'][i],
                                p['ssm_log_dt'][i], p['ssm_b_re'][i], p['ssm_b_im'][i], p['ssm_c_re'][i],
                                p['ssm_c_im'][i], p['ssm_d'][i], p['w_glu'][i], p['b_glu'][i])
            new_h.append(h_last)
        else:
            j = layer - N_A_LAYERS
            x = layer_b(x, k_all, v_all, q_offset, mem_k[layer], mem_v[layer], p['w_in_b'][j],
                        p['w_out_b'][j], p['g_pre_b'][j], p['g_post_b'][j])
    return x, jnp.stack(new_h), k_new, v_new

def setup_inputs(seed: int = 0) -> dict:
    key = jax.random.key(seed)
    ks = jax.random.split(key, 32)
    f32 = jnp.float32
    nrm = lambda k, shape, s=1.0: (jax.random.normal(k, shape, f32) * s).astype(f32)
    lam_im0 = jnp.pi * jnp.arange(SSM_STATE, dtype=f32)
    return {
        'x_prompt': nrm(ks[0], (BATCH, SEQ, D_MODEL)),
        'x_sample': nrm(ks[1], (DEC_BATCH, DEC_SEQ, D_MODEL)),
        'cache_k': nrm(ks[2], (DEC_BATCH, PAST_LEN, SB_HEADS, SB_HEAD_DIM)),
        'cache_v': nrm(ks[3], (DEC_BATCH, PAST_LEN, SB_HEADS, SB_HEAD_DIM)),
        'cache_mem_k': nrm(ks[4], (DEPTH, DEC_BATCH, N_MEM, MEM_HEADS, MEM_HEAD_DIM)),
        'cache_mem_v': nrm(ks[5], (DEPTH, DEC_BATCH, N_MEM, MEM_HEADS, MEM_HEAD_DIM)),
        'state_ssm': nrm(ks[6], (N_A_LAYERS, DEC_BATCH, SSM_GROUPS, SSM_STATE, 2), 0.1),
        'mem_prompt': nrm(ks[7], (BATCH, N_MEM, D_MODEL)),
        'w_in_a': nrm(ks[8], (N_A_LAYERS, D_MODEL, IN_WIDTH), D_MODEL ** -0.5),
        'w_out_a': nrm(ks[9], (N_A_LAYERS, OUT_WIDTH, D_MODEL), OUT_WIDTH ** -0.5),
        'g_pre_a': 1.0 + nrm(ks[10], (N_A_LAYERS, D_MODEL), 0.02),
        'g_post_a': 1.0 + nrm(ks[11], (N_A_LAYERS, D_MODEL), 0.02),
        'ssm_lam_re': -0.5 + nrm(ks[12], (N_A_LAYERS, SSM_GROUPS, SSM_STATE), 0.01),
        'ssm_lam_im': lam_im0 + nrm(ks[13], (N_A_LAYERS, SSM_GROUPS, SSM_STATE), 0.01),
        'ssm_log_dt': jax.random.uniform(ks[14], (N_A_LAYERS, SSM_GROUPS), f32, math.log(DT_MIN), math.log(DT_MAX)),
        'ssm_b_re': nrm(ks[15], (N_A_LAYERS, SSM_GROUPS, SSM_STATE, SSM_GROUP), (2 * SSM_GROUP) ** -0.5),
        'ssm_b_im': nrm(ks[16], (N_A_LAYERS, SSM_GROUPS, SSM_STATE, SSM_GROUP), (2 * SSM_GROUP) ** -0.5),
        'ssm_c_re': nrm(ks[17], (N_A_LAYERS, SSM_GROUPS, SSM_GROUP, SSM_STATE), (2 * SSM_STATE) ** -0.5),
        'ssm_c_im': nrm(ks[18], (N_A_LAYERS, SSM_GROUPS, SSM_GROUP, SSM_STATE), (2 * SSM_STATE) ** -0.5),
        'ssm_d': nrm(ks[19], (N_A_LAYERS, SSM_GROUPS, SSM_GROUP)),
        'w_glu': nrm(ks[20], (N_A_LAYERS, MIX_WIDTH, MIX_WIDTH), MIX_WIDTH ** -0.5),
        'b_glu': nrm(ks[21], (N_A_LAYERS, MIX_WIDTH), 0.01),
        'g_kv': 1.0 + nrm(ks[22], (D_MODEL,), 0.02),
        'w_kv': nrm(ks[23], (D_MODEL, 2 * MIX_WIDTH), D_MODEL ** -0.5),
        'w_in_b': nrm(ks[24], (N_B_LAYERS, D_MODEL, IN_WIDTH), D_MODEL ** -0.5),
        'w_out_b': nrm(ks[25], (N_B_LAYERS, OUT_WIDTH, D_MODEL), OUT_WIDTH ** -0.5),
        'g_pre_b': 1.0 + nrm(ks[26], (N_B_LAYERS, D_MODEL), 0.02),
        'g_post_b': 1.0 + nrm(ks[27], (N_B_LAYERS, D_MODEL), 0.02),
        'w_mem_k': nrm(ks[28], (DEPTH, D_MODEL, MEM_WIDTH), D_MODEL ** -0.5),
        'w_mem_v': nrm(ks[29], (DEPTH, D_MODEL, MEM_WIDTH), D_MODEL ** -0.5),
    }

def reference(x_prompt, x_sample, cache_k, cache_v, cache_mem_k, cache_mem_v, state_ssm, mem_prompt,
              w_in_a, w_out_a, g_pre_a, g_post_a, ssm_lam_re, ssm_lam_im, ssm_log_dt, ssm_b_re, ssm_b_im,
              ssm_c_re, ssm_c_im, ssm_d, w_glu, b_glu, g_kv, w_kv, w_in_b, w_out_b, g_pre_b, g_post_b,
              w_mem_k, w_mem_v):
    p = dict(w_in_a=w_in_a, w_out_a=w_out_a, g_pre_a=g_pre_a, g_post_a=g_post_a, ssm_lam_re=ssm_lam_re,
             ssm_lam_im=ssm_lam_im, ssm_log_dt=ssm_log_dt, ssm_b_re=ssm_b_re, ssm_b_im=ssm_b_im,
             ssm_c_re=ssm_c_re, ssm_c_im=ssm_c_im, ssm_d=ssm_d, w_glu=w_glu, b_glu=b_glu, g_kv=g_kv,
             w_kv=w_kv, w_in_b=w_in_b, w_out_b=w_out_b, g_pre_b=g_pre_b, g_post_b=g_post_b)
    bp = x_prompt.shape[0]
    mem_k_prompt = jnp.einsum('bmd,lde->lbme', mem_prompt, w_mem_k).reshape(DEPTH, bp, N_MEM, MEM_HEADS, MEM_HEAD_DIM)
    mem_v_prompt = jnp.einsum('bmd,lde->lbme', mem_prompt, w_mem_v).reshape(DEPTH, bp, N_MEM, MEM_HEADS, MEM_HEAD_DIM)
    h0_prompt = jnp.zeros((N_A_LAYERS, bp, SSM_GROUPS, SSM_STATE), jnp.complex64)
    y_prompt, h_prompt, k_prompt, v_prompt = trunk(x_prompt, mem_k_prompt, mem_v_prompt, h0_prompt,
                                                   None, None, 0, p)
    h0_sample = lax.complex(state_ssm[..., 0].astype(jnp.float32), state_ssm[..., 1].astype(jnp.float32))
    y_sample, h_sample, k_sample, v_sample = trunk(x_sample, cache_mem_k, cache_mem_v, h0_sample,
                                                   cache_k, cache_v, cache_k.shape[1], p)
    ssm_prompt = jnp.stack([jnp.real(h_prompt), jnp.imag(h_prompt)], axis=-1).astype(x_prompt.dtype)
    ssm_sample = jnp.stack([jnp.real(h_sample), jnp.imag(h_sample)], axis=-1).astype(state_ssm.dtype)
    return (y_prompt, y_sample, k_prompt, v_prompt, k_sample, v_sample, ssm_prompt, ssm_sample,
            mem_k_prompt, mem_v_prompt)


_drawn_inputs = setup_inputs


def setup_inputs(seed=0):
    import zlib

    import numpy as np

    out = dict(_drawn_inputs(seed))
    spreads = {}
    factors = {'g_post_a': 3.363,
     'ssm_lam_re': 4.282,
     'b_glu': 8.0,
     'g_kv': 2.818,
     'g_pre_b': 4.413,
     'g_post_b': 4.891}
    for name, (base, spread) in spreads.items():
        noise = np.random.default_rng([zlib.crc32(name.encode()), seed]).standard_normal(out[name].shape)
        drawn = base * np.exp(spread * noise) if base else spread * noise
        out[name] = __import__('jax').numpy.asarray(drawn.astype(out[name].dtype))
    for name, factor in factors.items():
        out[name] = (out[name] * factor).astype(out[name].dtype)
    return out
```

```python
from contextlib import ExitStack
import math

import concourse.bass as bass
from concourse import mybir

F32 = mybir.dt.float32
F32R = mybir.dt.float32r
I32 = mybir.dt.int32
ALU = mybir.AluOpType
ACT = mybir.ActivationFunctionType
AX = mybir.AxisListType
ds = bass.ds

P = 128
D = 2048
KT = D // P
SEQ, NB, DSEQ, PAST = 512, 8, 16, 128
NT = SEQ // P + 1
TOK = NT * P
HALF = TOK // 2
MIX, MEMW = 1536, 512
MIXB = MIX // P
NBLK = (2 * MIX + 2 * MEMW) // P
MH, NM = 4, 256
HEADS = MIX // P
EPS = 1e-6
SCALE = 1.0 / math.sqrt(P)
G, ST, GH = 96, 64, 16
PAIRS = G // 2
STEPS = 8
NC = TOK // STEPS
PC = SEQ // STEPS
JB = 8
BATCHES = PAIRS // JB
CW = 256
RW = 512
LEAD = 3
RING = 4
NPW = 23


class Order:

    def __init__(self, eng, sem):
        self.eng, self.sem, self.n, self.start = eng, sem, 0, None

    def __call__(self, ins):
        ins.then_inc(self.sem, 1)
        self.n += 1
        return ins

    def count(self):
        return self.n if self.start is None else self.start[1] * self.start[2] + self.n

    def wait(self):
        self.eng.wait_ge(self.sem, self.count())

    def enter(self, i, per):
        self.start = (self.n, i, per)

    def leave(self, times):
        base, i, per = self.start
        assert self.n - base == per, (self.n - base, per)
        self.n = base + per * times
        self.start = None


def build(nc, io, out, scr):
    with ExitStack() as ctx:
        def sb(name, shape, dt=F32):
            return ctx.enter_context(nc.sbuf_tensor(name, shape, dt))

        def sem(name):
            return ctx.enter_context(nc.semaphore(name))

        ctx.enter_context(nc.allow_non_contiguous_dma(reason="small tables and states"))
        XH, XL = sb("XH", [P, KT, TOK], F32R), sb("XL", [P, KT, TOK], F32R)
        RAW = sb("RAW", [P, 2, 1024])
        WH, WL = sb("WH", [P, RING, 1024], F32R), sb("WL", [P, RING, 1024], F32R)
        EST = sb("EST", [P, 2, TOK])
        ident, tri, ones = sb("ident", [P, P]), sb("tri", [P, P]), sb("ones", [P, P])
        vec = sb("vec", [P, 64])
        ss, rstd, nhalf = sb("ss", [P, 32]), sb("rstd", [P, 32]), sb("nhalf", [P, 1])
        marks = sb("marks", [1, 40])
        FN = 20640
        FA = sb("FA", [P, FN])
        PS = ctx.enter_context(nc.psum_tensor("PS", [P, 8, 512], F32))

        def place(shapes, at=0):
            views = []
            for shape in shapes:
                n = int(math.prod(shape))
                v = FA[:, at:at + n]
                names = "abcde"[:len(shape)]
                if len(shape) > 1:
                    v = v.rearrange("p (" + " ".join(names) + ") -> p " + " ".join(names),
                                    **{names[k]: shape[k] for k in range(len(shape))})
                views.append(v)
                at += n
            assert at <= FN, at
            return views

        class Phase:
            def __init__(self, name, w, units, kts, cw, gcol, first):
                self.name, self.w, self.kts, self.cw, self.gcol, self.first = name, w, kts, cw, gcol, first
                self.upc, self.units = units, None

        phases = {}
        at = 0
        for name, w, kts, cw, gcol, chunks, upc in (
                ("mem", None, 2, RW, None, 4, 8),
                ("in_a", io["w_in_a"][0], 4, CW, 0, 16, 4),
                ("glu", io["w_glu"][0], 3, CW, None, 6, 4),
                ("out_a", io["w_out_a"][0], 2, RW, None, 4, 8),
                ("kv", io["w_kv"], 2, RW, 16, 6, 8),
                ("in_b", io["w_in_b"][0], 4, CW, 32, 16, 4),
                ("out_b", io["w_out_b"][0], 2, RW, None, 4, 8)):
            phases[name] = Phase(name, w, upc, kts, cw, gcol, at)
            phases[name].chunks = chunks
            at += chunks * upc
        UNITS = at
        TABLE = []
        for ph in phases.values():
            TABLE += [(ph, k) for c in range(ph.chunks) for k in range(ph.upc)]

        def wview(t, slot, ph):
            return t[:, slot, 0:ph.kts * ph.cw].rearrange("p (k c) -> p k c", k=ph.kts)

        s_ld = [sem(f"weights_loaded{k}") for k in range(2)]
        s_wh, s_wl, s_wu = sem("weights_high"), sem("weights_low"), sem("weights_used")

        def load_unit(eng, ph, U, k, src):
            par = k % 2
            if not (isinstance(U, int) and U < 2):
                eng.wait_ge(s_wl, U - 1)
                eng.wait_ge(s_wh, U - 1)
            eng.dma_start(wview(RAW, par, ph), src).then_inc(s_ld[par], 16)

        def split_high(eng, ph, U, k):
            par, slot = k % 2, k % RING
            eng.wait_ge(s_ld[par], (U - par) * 8 + 16)
            if not (isinstance(U, int) and U < RING):
                eng.wait_ge(s_wu, U - RING + 1)
            if ph.gcol is None:
                n = ph.kts * ph.cw
                eng.activation(WH[:, slot, 0:n], RAW[:, par, 0:n], ACT.Copy).then_inc(s_wh, 1)
            else:
                for kt in range(ph.kts):
                    g = ph.gcol + (k % ph.upc) * ph.kts + kt
                    ins = eng.activation(wview(WH, slot, ph)[:, kt, :], wview(RAW, par, ph)[:, kt, :], ACT.Copy,
                                         scale=vec[:, g:g + 1])
                ins.then_inc(s_wh, 1)

        def split_low(eng, ph, U, k):
            par, slot = k % 2, k % RING
            eng.wait_ge(s_wh, U + 1)
            n = ph.kts * ph.cw
            if ph.gcol is None:
                eng.tensor_tensor(WL[:, slot, 0:n], RAW[:, par, 0:n], WH[:, slot, 0:n].bitcast(F32),
                                  ALU.subtract).then_inc(s_wl, 1)
            else:
                for kt in range(ph.kts):
                    g = ph.gcol + (k % ph.upc) * ph.kts + kt
                    ins = eng.scalar_tensor_tensor(
                        out=wview(WL, slot, ph)[:, kt, :], in0=wview(RAW, par, ph)[:, kt, :],
                        scalar=vec[:, g:g + 1], in1=wview(WH, slot, ph)[:, kt, :].bitcast(F32),
                        op0=ALU.mult, op1=ALU.subtract)
                ins.then_inc(s_wl, 1)

        def ahead(split, eng, ph, U, k):
            if isinstance(U, int):
                if U + LEAD < UNITS:
                    nph, nk = TABLE[U + LEAD]
                    split(eng, nph, U + LEAD, nk)
            else:
                split(eng, ph, U + LEAD, (k + LEAD) % ph.upc)

        def three(pe, acc, wh, wl, xh, xl, first, last):
            pe.matmul(acc, wh, xh, start=first, stop=False)
            pe.matmul(acc, wh, xl, start=False, stop=False)
            return pe.matmul(acc, wl, xh, start=False, stop=last)

        s_memset = sem("constants_set")
        s_vecd, s_vect, s_vec = sem("vector_rows_loaded"), sem("vector_rows_turned"), sem("vectors_ready")
        s_act, s_dve, s_pool = sem("scalar_steps"), sem("vector_steps"), sem("gpsimd_steps")
        s_rowd = [sem(f"row_loaded{k}") for k in range(2)]
        s_row = sem("row_normalised")
        s_xt, s_xh, s_xl = sem("rows_turned"), sem("turned_high"), sem("turned_low")
        s_sq, s_rs = sem("squares_summed"), sem("rstd_ready")
        s_bank = {n: sem(f"bank_full_{n}") for n in phases}
        s_ev = {n: sem(f"bank_emptied_{n}") for n in phases}
        s_st = {n: [sem(f"stage_stored_{n}{k}") for k in range(2)] for n in ("mem", "in_a", "in_b")}
        s_par, s_parT, s_parE = sem("params_loaded"), sem("params_turned"), sem("params_copied")
        s_zero = sem("zeros_set")
        s_trig, s_sin, s_pw = sem("angles_ready"), sem("sines_ready"), sem("powers_ready")

        ROW, JUNK = place([(2, D), (D,)])
        OUTROW, GB, JUNK2, ss4 = place([(NT, D), (D,), (RW,), (2, NT, 4)], at=2 * D)
        (U, CR, SR, CTH, W, FS, FO, KDS, BVT, TZ, HPZ, PW, PB, BR, BV, TMP, CP, BB, DT, KA, DTS) = place(
            [(2 * JB, NC), (2, P), (2 * P,), (384,), (2, JB, NC), (2, NB + 1, JB), (2 * P,), (JB, P), (2 * JB * P,),
             (2 * JB, P), (2, 2, JB, NC), (NPW, 2, PAIRS), (NPW, 2, JB), (2, JB, GH), (2, JB, STEPS, GH),
             (JB * (STEPS + 1) * GH,), (2, JB, STEPS + 1, GH), (2, JB, 2, GH), (G,), (6, 2, JB), (2 * JB,)])

        def x_rows(t):
            if t < NT - 1:
                return io["x_prompt"][0, P * t:P * t + P, :].rearrange("(c s) d -> s c d", s=STEPS)
            return io["x_sample"].rearrange("b (k s) d -> s (b k) d", s=STEPS)

        def x_rows_plain(t):
            if t < NT - 1:
                return io["x_prompt"][0, P * t:P * t + P, :]
            return io["x_sample"].rearrange("b i d -> (b i) d")


        VROW = JUNK[:, 0:P]
        PRM = TMP[:, 0:384].rearrange("p (a m) -> p a m", a=3)
        PRL, DRW, PRD = TMP[:, 384:386], TMP[:, 400:416], TMP[:, 512:640]
        CPF = CP.rearrange("p a b c d -> p (a b c d)")
        WV = BVT
        KST = BVT[:, :].rearrange("p (x j c) -> p x j c", x=4, j=JB)
        YS = W[:, :, :, :].rearrange("p r j c -> p (r j) c")

        def CPT(k, n=1):
            return CPF[:, PAIRS * k:PAIRS * (k + n)]

        s_u, s_crd, s_brd = sem("u_loaded"), sem("c_rows_loaded"), sem("b_loaded")
        s_cT, s_cTe = sem("c_turned"), sem("c_copied")
        s_bv, s_cp, s_bb = sem("bv_ready"), sem("cp_ready"), sem("b_blocks_ready")
        s_wvT, s_wve = sem("wv_turned"), sem("wv_copied")
        s_V, s_Ve = sem("v_products"), sem("v_copied")
        s_kd, s_kde, s_kst, s_tz = sem("lags_product"), sem("lags_copied"), sem("lags_stored"), sem("tz_loaded")
        s_hp, s_fs, s_fT, s_fTe, s_fst = sem("states_ready"), sem("finals_ready"), sem("finals_turned"), sem("finals_copied"), sem("finals_stored")
        s_y, s_ye, s_yst = sem("y_products"), sem("y_ready"), sem("y_stored")

        def prime_ssm(pool):
            for k, (s, n) in enumerate(((s_ye, 3), (s_y, 3), (s_wvT, 1), (s_kd, 1), (s_cp, 1), (s_hp, 1), (s_cT, 1),
                         (s_fT, 1), (s_fTe, 1), (s_yst, 128), (s_fst, 32), (s_kst, 16), (s_kde, 1), (s_bb, 1))):
                pool.memset(marks[0:1, k + 1:k + 2], 0.0).then_inc(s, n)

        def ssm_params(dve, mine):
            dve.wait_ge(s_par, 64)
            mine(dve.tensor_copy(PRM[0:48, 2, :].rearrange("j (q p) -> j q p", q=2),
                                 PRL[0:48, :].unsqueeze(2).broadcast_to([48, 2, ST])))
            dve.tensor_copy(PRD[0:G, :].rearrange("g (t h) -> g t h", h=GH),
                            DRW[0:G, :].unsqueeze(1).broadcast_to([G, STEPS, GH])).then_inc(s_parE, 1)

        def ssm_params2(dve, mine):
            def step(ins):
                mine(ins)
                mine.wait()

            ts, tt, stt = dve.tensor_scalar, dve.tensor_tensor, dve.scalar_tensor_tensor

            def nearest(o, x, factor):
                step(ts(o, x, factor, 12582912.0, ALU.mult, ALU.add))
                step(ts(o, o, -12582912.0, None, ALU.add))

            def exp(o, x, k, r):
                step(ts(x, x, -87.0, 88.0, ALU.max, ALU.min))
                nearest(k, x, 1.4426950408889634)
                step(stt(out=r, in0=k, scalar=-0.693359375, in1=x, op0=ALU.mult, op1=ALU.add))
                step(stt(out=r, in0=k, scalar=2.12194440054690583e-4, in1=r, op0=ALU.mult, op1=ALU.add))
                step(ts(o, r, 1.0 / 5040, None, ALU.mult))
                for n in (720, 120, 24, 6, 2, 1):
                    step(stt(out=o, in0=o, scalar=1.0 / n, in1=r, op0=ALU.add, op1=ALU.mult))
                step(ts(k.bitcast(I32), k, 127.0, 8388608.0, ALU.add, ALU.mult))
                step(stt(out=o, in0=o, scalar=1.0, in1=k, op0=ALU.add, op1=ALU.mult))

            dve.wait_ge(s_parT, 1)
            mine(dve.tensor_copy(CPT(0, 3), PS[:, 7, 64:64 + 144]))
            step(dve.tensor_copy(DT, PS[:, 7, 208:208 + G]))
            lre, lim, ldt, dt, mag, ang, kk, r, rc, ra = (CPT(k) for k in (0, 1, 2, 3, 5, 6, 7, 8, 10, 9))
            exp(dt, ldt, kk, r)
            step(tt(CPT(4), lre, dt, ALU.mult))
            exp(mag, CPT(4), kk, r)
            step(tt(ang, lim, dt, ALU.mult))
            nearest(kk, ang, 1.0 / (2 * math.pi))
            step(stt(out=r, in0=kk, scalar=-6.28125, in1=ang, op0=ALU.mult, op1=ALU.add))
            step(stt(out=r, in0=kk, scalar=-0.0019350051879882812, in1=r, op0=ALU.mult, op1=ALU.add))
            step(stt(out=r, in0=kk, scalar=-3.0199157e-07, in1=r, op0=ALU.mult, op1=ALU.add))
            step(ts(r, r, -3.1415925, 3.1415925, ALU.max, ALU.min))
            step(stt(out=ra, in0=r, scalar=-1.0, in1=r, op0=ALU.mult, op1=ALU.max))
            dve.tensor_scalar(rc, ra, -1.0, math.pi / 2, ALU.mult, ALU.add).then_inc(s_trig, 1)

        def ssm_params3(dve, mine):
            def step(ins):
                mine(ins)
                mine.wait()

            ts, tt, stt = dve.tensor_scalar, dve.tensor_tensor, dve.scalar_tensor_tensor
            lre, lim, mag, sin, cos = (CPT(k) for k in (0, 1, 5, 11, 12))
            dve.wait_ge(s_sin, 1)
            step(tt(PW[:, 1, 0, :], mag, cos, ALU.mult))
            step(tt(PW[:, 1, 1, :], mag, sin, ALU.mult))
            step(dve.memset(PW[:, 0, 0, :], 1.0))
            step(dve.memset(PW[:, 0, 1, :], 0.0))
            nr, ni, den, t1, t2 = PW[:, 2, 0, :], PW[:, 1, 1, :], CPT(13), CPT(14), CPT(15)
            step(ts(nr, PW[:, 1, 0, :], -1.0, None, ALU.add))
            step(tt(t1, lre, lre, ALU.mult))
            step(tt(t2, lim, lim, ALU.mult))
            step(tt(den, t1, t2, ALU.add))
            step(dve.reciprocal(den, den))
            step(tt(t1, nr, lre, ALU.mult))
            step(tt(t2, ni, lim, ALU.mult))
            step(tt(t1, t1, t2, ALU.add))
            step(tt(CPT(16), t1, den, ALU.mult))
            step(tt(t1, ni, lre, ALU.mult))
            step(tt(t2, nr, lim, ALU.mult))
            step(tt(t1, t1, t2, ALU.subtract))
            dve.tensor_tensor(CPT(17), t1, den, ALU.mult).then_inc(s_pw, 1)

        def complex_product(eng, mine, dst, a, b, t, ready=None):
            tt = eng.tensor_tensor
            mine(tt(dst[0], a[0], b[0], ALU.mult))
            mine(tt(t, a[1], b[1], ALU.mult))
            mine.wait()
            mine(tt(dst[0], dst[0], t, ALU.subtract))
            mine.wait()
            mine(tt(dst[1], a[0], b[1], ALU.mult))
            mine(tt(t, a[1], b[0], ALU.mult))
            mine.wait()
            if ready is not None:
                tt(dst[1], dst[1], t, ALU.add).then_inc(ready, 1)
                return
            mine(tt(dst[1], dst[1], t, ALU.add))
            mine.wait()

        def ssm_params_pool(pool, mine):
            pool.wait_ge(s_pw, 1)

            def both(a, b):
                return PW[:, a:b, 0, :], PW[:, a:b, 1, :]

            def repeated(v, n):
                return tuple(x.broadcast_to([P, n, PAIRS]) for x in v)

            t = TMP[:, 0:384].rearrange("p (k j) -> p k j", k=8)
            complex_product(pool, mine, both(2, 3), both(1, 2), both(1, 2), t[:, 0:1, :])
            complex_product(pool, mine, both(3, 5), both(1, 3), repeated(both(2, 3), 2), t[:, 0:2, :])
            complex_product(pool, mine, both(5, 9), both(1, 5), repeated(both(4, 5), 4), t[:, 0:4, :])
            q = tuple(CPT(k).unsqueeze(1).broadcast_to([P, 8, PAIRS]) for k in (16, 17))
            back = tuple(PW[:, 7::-1, k, :] for k in range(2))
            complex_product(pool, mine, both(9, 17), back, q, t)
            mine(pool.tensor_copy(PW[:, 17, :, :], PW[:, 8, :, :]))
            mine.wait()
            for k in range(17, 22):
                complex_product(pool, mine, both(k + 1, k + 2), both(k, k + 1), both(k, k + 1), t[:, 0:1, :])

        def ssm_pool(pool, mine, i):
            pool.wait_ge(s_cT, i + 1)
            pool.wait_ge(s_memset, 1)
            for q in range(2):
                for j, name in enumerate(("ssm_c_re", "ssm_c_im")):
                    src = io[name][0].rearrange("(x j q) h p -> x q j h p", q=2, j=JB)[ds(i, 1), q].rearrange("o j h p -> (o j) h p")
                    pool.dma_start(CR[:, j, q * ST:q * ST + ST], src).then_inc(s_crd, 16)
            src = io["state_ssm"][0].rearrange("b (x j q) p r -> x b j (q p r)", q=2, j=JB)[ds(i, 1)].rearrange("o b j f -> (o b) j f")
            pool.dma_start(SR[0:64, :], src).then_inc(s_crd, 16)
            for j, name in enumerate(("ssm_b_re", "ssm_b_im")):
                src = io[name][0].rearrange("(x j q) p h -> x (q p) j h", q=2, j=JB)[ds(i, 1)].rearrange("o m j h -> (o m) j h")
                pool.dma_start(BR[:, j, :, :], src).then_inc(s_brd, 16)
            mine(pool.tensor_copy(PB[:], PW[:, :, :, ds(i * JB, JB)]))
            mine.wait()
            pool.wait_ge(s_brd, i * 32 + 32)
            pool.wait_ge(s_wvT, i + 1)
            pool.wait_ge(s_bb, i + 1)
            full = [P, JB, STEPS, GH]
            b = tuple(BR[:, k, :, :].unsqueeze(2).broadcast_to(full) for k in range(2))
            qa = tuple(PB[:, 9:17, k, :].rearrange("p s j -> p j s").unsqueeze(3).broadcast_to(full) for k in range(2))
            t = TMP[:, 0:JB * STEPS * GH].rearrange("p (j s h) -> p j s h", j=JB, s=STEPS)
            complex_product(pool, mine, (BV[:, 0], BV[:, 1]), b, qa, t, s_bv)
            pool.wait_ge(s_bv, i + 1)
            pool.wait_ge(s_cTe, i + 1)
            pool.wait_ge(s_y, i * 3 + 3)
            full = [P, JB, STEPS + 1, GH]
            c = tuple(CTH[:, k * P:(k + 1) * P].rearrange("p (j h) -> p j h", h=GH).unsqueeze(2).broadcast_to(full) for k in range(2))
            a = tuple(PB[:, 0:9, k, :].rearrange("p s j -> p j s").unsqueeze(3).broadcast_to(full) for k in range(2))
            t = TMP[:].rearrange("p (j s h) -> p j s h", j=JB, s=STEPS + 1)
            tt = pool.tensor_tensor
            mine(tt(CP[:, 0], c[0], a[0], ALU.mult))
            mine(tt(t, c[1], a[1], ALU.mult))
            mine.wait()
            mine(tt(CP[:, 0], CP[:, 0], t, ALU.add))
            mine.wait()
            mine(tt(CP[:, 1], c[1], a[0], ALU.mult))
            mine(tt(t, c[0], a[1], ALU.mult))
            mine.wait()
            pool.tensor_tensor(CP[:, 1], CP[:, 1], t, ALU.subtract).then_inc(s_cp, 1)

        def ssm_pe(pe, ph, i):
            def turn_c():
                pe.wait_ge(s_crd, i * 80 + 80)
                pe.wait_ge(s_ye, i * 3 + 3)
                for k in range(2):
                    pe.transpose(PS[:, 4, k * P:k * P + P], CR[:, k, :], ident[:])
                for k in range(2):
                    ins = pe.transpose(PS[:, 4, 256 + 64 * k:320 + 64 * k],
                                       SR[0:64, :].rearrange("b (m r) -> b r m", r=2)[:, k, :], ident[0:64, 0:64])
                ins.then_inc(s_cT, 1)

            def turn_bv():
                pe.wait_ge(s_bv, i + 1)
                pe.wait_ge(s_cTe, i + 1)
                pe.wait_ge(s_fTe, i + 1)
                for x in range(4):
                    for j in range(4):
                        r, jj = x // 2, 4 * (x % 2) + j
                        ins = pe.transpose(PS[:, 4 + x, j * P:j * P + P], BV[:, r, jj].rearrange("p s h -> p (s h)"), ident[:])
                ins.then_inc(s_wvT, 1)

            def products_v(part):
                if part == 0:
                    pe.wait_ge(s_u, i * 128 + 128)
                    pe.wait_ge(s_wve, i * 4 + 4)
                else:
                    pe.wait_ge(s_Ve, i * 2 + 1)
                for j in range(4):
                    jj = 4 * part + j
                    for r in range(2):
                        for q in range(2):
                            c = r * 160 + q * 80
                            ins = pe.matmul(PS[:, 4 + j, c:c + NC], WV[:, (r * JB + jj) * P:(r * JB + jj + 1) * P],
                                            U[:, 2 * jj + q, :], start=(c == 0), stop=True, skip_group_check=True)
                ins.then_inc(s_V, 1)

            def products_lags():
                pe.wait_ge(s_cp, i + 2)
                pe.wait_ge(s_bb, i + 2)
                pe.wait_ge(s_Ve, i * 2 + 2)
                for j in range(JB):
                    o = PS[0:32, 4 + j // 4, (j % 4) * P:(j % 4 + 1) * P]
                    for r in range(2):
                        ins = pe.matmul(o, BB[:, r, j].rearrange("p q h -> p (q h)"),
                                        CP[:, r, j, 0:8].rearrange("p k h -> p (k h)"),
                                        start=(r == 0 and j % 4 == 0), stop=(r == 1), skip_group_check=True)
                ins.then_inc(s_kd, 1)

            def products_y():
                pe.wait_ge(s_tz, i * 128 + 128)
                pe.wait_ge(s_hp, i + 2)
                pe.wait_ge(s_kde, i + 2)
                for g in range(2 * JB):
                    j, q = g // 2, g % 2
                    o = PS[:, 4 + g // 6, (g % 6) * NC:(g % 6 + 1) * NC]
                    pe.matmul(o, TZ[:, g, :], U[:, g, :], start=(g % 6 == 0), stop=False, skip_group_check=True)
                    for r in range(2):
                        ins = pe.matmul(o, CP[:, r, j, 1:9].rearrange("p k h -> p (k h)"), HPZ[:, r, q, j, :],
                                        start=False, stop=(r == 1), skip_group_check=True)
                    if g in (5, 11, 15):
                        ins.then_inc(s_y, 1)
                pe.wait_ge(s_fs, i + 1)
                for r in range(2):
                    ins = pe.transpose(PS[0:72, 7, r * P:r * P + P], FS[:, r].rearrange("p b j -> p (b j)"), ident[:])
                ins.then_inc(s_fT, 1)

            aux = {0: [turn_c], 1: [turn_bv], 3: [lambda: products_v(0), lambda: products_v(1)], 4: [products_lags]}
            for x in range(8):
                for f in aux.get(x, ()):
                    f()
                n = i * 2 + 1 + x // 4
                unit_stationary(pe, ph, (i * 2 + 1 + x // 4) * 4 + ph.first + x % 4, x % 4, n)
            products_y()

        def ssm_act(act, mine, i):
            def early():
                act.wait_ge(s_cT, i + 2)
                act.wait_ge(s_cp, i + 1)
                act.wait_ge(s_hp, i + 1)
                act.activation(CTH[:, 0:P], PS[:, 4, 0:P], ACT.Copy)
                act.activation(CTH[:, P:2 * P], PS[:, 4, P:2 * P], ACT.Copy, scale=-1.0)
                act.activation(CTH[:, 2 * P:384], PS[:, 4, 2 * P:384], ACT.Copy).then_inc(s_cTe, 1)

            def second():
                act.wait_ge(s_zero, 3)
                act.wait_ge(s_bv, i + 1)
                act.wait_ge(s_kd, i + 1)
                for q in range(2):
                    r = slice(q * ST, q * ST + ST)
                    ins = act.activation(BB[r, :, :, q, :], BV[r, :, :, STEPS - 1, :], ACT.Copy)
                ins.then_inc(s_bb, 1)
                for m in range(2):
                    act.wait_ge(s_st["in_a"][m], i * 32 + 16)
                act.wait_ge(s_ye, i * 3 + 3)
                src = scr["in_a"][ds(i * 2, 2)].rearrange("m (g h) (s c) -> s h (m g) c", h=GH, s=STEPS)
                for s in range(STEPS):
                    act.dma_start(U[s * GH:s * GH + GH, :, :], src[s]).then_inc(s_u, 16)
                act.wait_ge(s_wvT, i + 2)
                for x in range(4):
                    act.activation(WV[:, x * 512:(x + 1) * 512], PS[:, 4 + x, :], ACT.Copy).then_inc(s_wve, 1)

            def copy_v():
                for part in range(2):
                    act.wait_ge(s_V, i * 2 + 1 + part)
                    if part == 0:
                        act.wait_ge(s_yst, i * 128 + 128)
                    for j in range(4):
                        for q in range(2):
                            r = slice(q * ST, q * ST + ST)
                            ins = act.activation(W[r, :, 4 * part + j, :],
                                                 PS[r, 4 + j, 0:320].rearrange("p (r q c) -> p r q c", r=2, q=2)[:, :, q, :], ACT.Copy)
                    ins.then_inc(s_Ve, 1)

            def lags():
                act.wait_ge(s_kd, i + 2)
                act.wait_ge(s_kst, i * 16 + 16)
                for x in range(2):
                    ins = act.activation(KDS[0:32, 4 * x:4 * x + 4, :],
                                         PS[0:32, 4 + x, :].rearrange("p (j m) -> p j m", j=4), ACT.Copy)
                ins.then_inc(s_kde, 1)
                act.wait_ge(s_kde, i + 2)
                dst = scr["lags"].rearrange("(x j q) h m -> x (q h) j m", j=JB, q=2)[ds(i, 1)].rearrange("o a j m -> (o a) j m")
                act.dma_start(dst, KDS[0:32]).then_inc(s_kst, 16)

            def spread_lags():
                act.wait_ge(s_zero, 3)
                act.wait_ge(s_kst, i * 16 + 32)
                act.wait_ge(s_y, i * 3 + 3)
                src = scr["lags"].rearrange("(x g) h m -> x h g m", g=2 * JB)[ds(i, 1)].rearrange("o h g m -> (o h) g m")
                for s in range(STEPS):
                    act.dma_start(TZ[s * GH:s * GH + GH, :, s * GH:P], src[:, :, 0:P - s * GH]).then_inc(s_tz, 16)

            def late():
                act.wait_ge(s_fT, i + 2)
                act.wait_ge(s_fst, i * 32 + 32)
                act.activation(FO[0:72, :].rearrange("b (m r) -> b r m", r=2),
                               PS[0:72, 7, 0:2 * P].rearrange("b (r m) -> b r m", r=2), ACT.Copy).then_inc(s_fTe, 1)
                act.wait_ge(s_fTe, i + 2)
                dst = out["ssm_sample"][0].rearrange("b (x j q) p r -> x b j (q p r)", q=2, j=JB)[ds(i, 1)].rearrange("o b j f -> (o b) j f")
                act.dma_start(dst, FO[0:64, :]).then_inc(s_fst, 16)
                dst = out["ssm_prompt"][0, 0].rearrange("(x j q) p r -> x j (q p r)", q=2, j=JB)[ds(i, 1)].rearrange("o j f -> (o j) f")
                act.dma_start(dst, FO[64:72, :]).then_inc(s_fst, 16)
                act.wait_ge(s_ye, i * 3 + 6)
                dst = scr["y"].rearrange("(x g) h (t c) -> x t h g c", g=2 * JB, t=STEPS)[ds(i, 1)].rearrange("o t h g c -> (o t) h g c")
                for t in range(STEPS):
                    act.dma_start(dst[t], YS[t * GH:t * GH + GH, :, :]).then_inc(s_yst, 16)

            return [early, second, None, copy_v, lags, spread_lags, None, None, late]

        def ssm_dve(dve, mine, i):
            tt = dve.tensor_tensor

            def level(lv):
                s = 1 << lv
                n = PC - s
                a = tuple(KA[:, lv, k, :].unsqueeze(2).broadcast_to([P, JB, n]) for k in range(2))
                old = tuple(W[:, k, :, 0:n] for k in range(2))
                t = [KST[:, k, :, 0:n] for k in range(4)]
                mine(tt(t[0], old[0], a[0], ALU.mult))
                mine(tt(t[1], old[1], a[1], ALU.mult))
                mine(tt(t[2], old[0], a[1], ALU.mult))
                mine(tt(t[3], old[1], a[0], ALU.mult))
                mine.wait()
                mine(tt(t[0], t[0], t[1], ALU.subtract))
                mine(tt(t[2], t[2], t[3], ALU.add))
                mine.wait()
                for k in range(2):
                    new = W[:, k, :, s:PC]
                    mine(tt(new, new, t[2 * k], ALU.add))
                mine.wait()

            def tables():
                mine(dve.tensor_copy(KA[:], PW[:, 17:23, :, ds(i * JB, JB)]))
                mine(dve.tensor_copy(DTS[:], DT[:, ds(i * 2 * JB, 2 * JB)]))
                mine.wait()

            def first():
                dve.wait_ge(s_Ve, i * 2 + 2)
                level(0)
                level(1)

            def second():
                level(2)
                level(3)

            def third():
                level(4)
                level(5)

            def fourth():
                a = tuple(KA[:, 0, k, :].unsqueeze(2).broadcast_to([P, JB, NB]) for k in range(2))
                sample = W[:, :, :, PC:NC].rearrange("p r j (b k) -> p r j b k", k=2)
                h0 = CTH[:, 2 * P:384].rearrange("p (r b j) -> p r j b", r=2, b=NB)
                t = [KST[:, k, :, 0:NB] for k in range(4)]
                for step in range(2):
                    h = [h0[:, r] if step == 0 else sample[:, r, :, :, 0] for r in range(2)]
                    mine(tt(t[0], h[0], a[0], ALU.mult))
                    mine(tt(t[1], h[1], a[1], ALU.mult))
                    mine(tt(t[2], h[0], a[1], ALU.mult))
                    mine(tt(t[3], h[1], a[0], ALU.mult))
                    mine.wait()
                    mine(tt(t[0], t[0], t[1], ALU.subtract))
                    mine(tt(t[2], t[2], t[3], ALU.add))
                    mine.wait()
                    for k in range(2):
                        new = sample[:, k, :, :, step]
                        mine(tt(new, new, t[2 * k], ALU.add))
                    mine.wait()
                dve.wait_ge(s_y, i * 3 + 3)
                dve.wait_ge(s_zero, 3)
                for q in range(2):
                    r = slice(q * ST, q * ST + ST)
                    dve.tensor_copy(HPZ[r, :, q, :, 1:PC], W[r, :, :, 0:PC - 1])
                    new = HPZ[r, :, q, :, PC:NC].rearrange("p r j (b k) -> p r j b k", k=2)
                    dve.tensor_copy(new[:, :, :, :, 0], h0[r])
                    for k in range(2):
                        ins = dve.tensor_copy(new[:, k, :, :, 1], sample[r, k, :, :, 0])
                ins.then_inc(s_hp, 1)
                dve.wait_ge(s_fT, i + 1)
                for k in range(2):
                    dve.tensor_copy(FS[:, k, 0:NB, :], sample[:, k, :, :, 1].rearrange("p j b -> p b j"))
                mine(dve.tensor_copy(FS[:, :, NB, :], W[:, :, :, PC - 1]))
                mine.wait()
                dve.wait_ge(s_u, i * 128 + 128)
                dve.tensor_tensor(YS, U[:], DTS[:].unsqueeze(2).broadcast_to([P, 2 * JB, NC]), ALU.mult).then_inc(s_fs, 1)
                dve.wait_ge(s_fs, i + 1)

            def late():
                for x, n in ((0, 6), (1, 6), (2, 4)):
                    dve.wait_ge(s_y, i * 3 + 4 + x)
                    o = YS[:, 6 * x:6 * x + n, :]
                    tt(o, o, PS[:, 4 + x, 0:n * NC].rearrange("p (g c) -> p g c", c=NC), ALU.add).then_inc(s_ye, 1)

            return [tables, None, None, None, first, second, third, fourth, late]

        MQ, MG, MS, KVR, KTM, QZ, PR, PT, sm = place([(MH, TOK), (MH, TOK), (MH, TOK), (4, 2, MEMW), (2, MH, NM), (MH, NB, P),
                                                  (MH, NM), (2, MH, P), (2, 4, MH)])
        MSEQ = [("K", 0), ("S", 0), ("S", 1), ("P", 0), ("A", 0), ("S", 2), ("P", 1), ("A", 1), ("S", 3), ("P", 2), ("A", 2)]
        MSEQ += [x for b in range(NB) for x in (("K", b + 1), ("s", b))] + [("P", 3), ("A", 3), ("P", 4), ("A", 4)]
        TURN = {x: n for n, x in enumerate([y for y in MSEQ if y[0] in "KP"])}
        PER_LAYER = {"q_loaded": 16, "g_loaded": 16, "gate_sigmoid": 1, "gate_ready": 1, "qz": 1, "rows0": 96, "rows1": 96,
                     "rows2": 80, "vp": 16, "turned": 14, "high_copied": 14, "low_copied": 14, "scores": 5, "negmax": 5,
                     "exps": 5, "probs": 5, "values": 4, "value_stream": 8, "gated": 5, "stored": 16}
        mm = {n: sem(f"mem_{n}") for n in PER_LAYER}

        def layer_wait(eng, l, name, count):
            eng.wait_ge(mm[name], l * PER_LAYER[name] + count)

        SRC = ("in_a", "in_b")
        DST = ("out_a", "out_b")

        MRAW = QZ[:].rearrange("p h b m -> p (h b m)")[:, 0:MH * TOK].rearrange("p (h n) -> p h n", h=MH)

        def mem_cols(v, t):
            return v[:, P * t:P * t + P]

        def natural(v):
            return v.rearrange("p (c s) -> p s c", s=STEPS)

        def by_step(v):
            return v.rearrange("p (s c) -> p s c", s=STEPS)

        def stream_cols(v, b):
            return v[:, DSEQ * b:DSEQ * b + DSEQ]

        def mem_pe(pe, l):

            def bank_pair(x):
                if TURN[x]:
                    layer_wait(pe, l, "high_copied", TURN[x])
                    layer_wait(pe, l, "low_copied", TURN[x])

            for x in MSEQ:
                kind, t = x
                if kind == "K":
                    layer_wait(pe, l, f"rows{t % 3}", 16 * (t // 3 + 1))
                    bank_pair(x)
                    for mt in range(2):
                        for h in range(MH):
                            ins = pe.transpose(PS[:, 6 + mt, h * P:h * P + P], KVR[:, t % 3, mt, h * P:h * P + P], ident[:])
                    ins.then_inc(mm["turned"], 1)
                elif kind == "S":
                    n = TURN[("K", 0)] + 1
                    layer_wait(pe, l, "high_copied", n)
                    layer_wait(pe, l, "low_copied", n)
                    if t == 0:
                        layer_wait(pe, l, "qz", 1)
                    if t >= 2:
                        layer_wait(pe, l, "exps", t - 1)
                    for h in range(MH):
                        ins = pe.matmul(PS[:, 4 - 2 * (t % 2) + h // 2, (h % 2) * NM:(h % 2 + 1) * NM], mem_cols(MQ[:, h, :], t),
                                        KTM[:, 0, h, :], start=(h % 2 == 0), stop=True, skip_group_check=True)
                    ins.then_inc(mm["scores"], 1)
                elif kind == "s":
                    n = TURN[("K", t + 1)] + 1
                    layer_wait(pe, l, "high_copied", n)
                    layer_wait(pe, l, "low_copied", n)
                    if t == 0:
                        layer_wait(pe, l, "exps", 3)
                    for h in range(MH):
                        ins = pe.matmul(PS[:, 4 + h // 2, (h % 2) * NM:(h % 2 + 1) * NM], QZ[:, h, t, :], KTM[:, (t + 1) % 2, h, :],
                                        start=(t == 0 and h % 2 == 0), stop=(t == NB - 1), skip_group_check=True)
                    if t == NB - 1:
                        ins.then_inc(mm["scores"], 1)
                elif kind == "P":
                    layer_wait(pe, l, "probs", t + 1)
                    bank_pair(x)
                    for mt in range(2):
                        for h in range(MH):
                            ins = pe.transpose(PS[:, 6 + mt, h * P:h * P + P], PR[:, h, mt * P:mt * P + P], ident[:])
                    ins.then_inc(mm["turned"], 1)
                else:
                    layer_wait(pe, l, "high_copied", TURN[("P", t)] + 1)
                    layer_wait(pe, l, "low_copied", TURN[("P", t)] + 1)
                    if t >= 2:
                        layer_wait(pe, l, "gated", t - 1)
                    if t < NT - 1:
                        layer_wait(pe, l, "vp", 16)
                        for h in range(MH):
                            for mt in range(2):
                                ins = pe.matmul(PS[:, t % 2, h * P:h * P + P], KVR[:, 3, mt, h * P:h * P + P], PT[:, mt, h, :],
                                                start=(h == 0 and mt == 0), stop=(mt == 1), skip_group_check=True)
                        ins.then_inc(mm["values"], 1)
                    else:
                        for b in range(NB):
                            n = NB + 1 + b
                            layer_wait(pe, l, f"rows{n % 3}", 16 * (n // 3 + 1))
                            for h in range(MH):
                                for mt in range(2):
                                    ins = pe.matmul(stream_cols(PS[:, 0, h * P:h * P + P], b), KVR[:, n % 3, mt, h * P:h * P + P],
                                                    stream_cols(PT[:, mt, h, :], b),
                                                    start=(b == 0 and h == 0 and mt == 0), stop=(mt == 1), skip_group_check=True)
                            ins.then_inc(mm["value_stream"], 1)

        def mem_act(act, mine, l):
            layer_wait(act, l, "g_loaded", 16)
            for h in range(MH):
                if l == 0:
                    ins = act.activation(natural(MS[:, h, :]), by_step(MG[:, h, :]), ACT.Sigmoid)
                else:
                    ins = act.activation(MS[:, h, :], MG[:, h, :], ACT.Sigmoid)
            ins.then_inc(mm["gate_sigmoid"], 1)
            for x in MSEQ:
                kind, t = x
                if kind == "K":
                    layer_wait(act, l, "turned", TURN[x] + 1)
                    act.activation(KTM[:, t % 2, :, 0:P], PS[:, 6, :].rearrange("p (h m) -> p h m", h=MH), ACT.Copy).then_inc(mm["high_copied"], 1)
                elif kind == "P":
                    layer_wait(act, l, "negmax", t + 1)
                    if t:
                        layer_wait(act, l, "turned", TURN[("P", t - 1)] + 1)
                    for h in range(MH):
                        ins = act.activation(PR[:, h, :], PS[:, 4 - 2 * (t % 2) + h // 2, (h % 2) * NM:(h % 2 + 1) * NM], ACT.Exp,
                                             bias=sm[:, t % 2, 1, h:h + 1], scale=SCALE, accum_out=sm[:, t % 2, 2, h:h + 1])
                    ins.then_inc(mm["exps"], 1)
                    layer_wait(act, l, "turned", TURN[x] + 1)
                    if t:
                        layer_wait(act, l, "values", t)
                    act.activation(PT[:, 0, :, :], PS[:, 6, :].rearrange("p (h m) -> p h m", h=MH), ACT.Copy).then_inc(mm["high_copied"], 1)

        def mem_dve(dve, mine, l):
            layer_wait(dve, l, "q_loaded", 16)
            if l == 0:
                for h in range(MH):
                    mine(dve.tensor_copy(natural(MQ[:, h, :]), by_step(MRAW[:, h, :])))
                mine.wait()
            mine(dve.memset(QZ[:], 0.0))
            mine.wait()
            for b in range(NB):
                c = slice(SEQ + DSEQ * b, SEQ + DSEQ * b + DSEQ)
                ins = dve.tensor_copy(QZ[:, :, b, DSEQ * b:DSEQ * b + DSEQ], MQ[:, :, c])
            ins.then_inc(mm["qz"], 1)
            layer_wait(dve, l, "gate_sigmoid", 1)
            for h in range(MH):
                if l == 0:
                    ins = dve.tensor_tensor(natural(MS[:, h, :]), by_step(MG[:, h, :]), natural(MS[:, h, :]), ALU.mult)
                else:
                    ins = dve.tensor_tensor(MS[:, h, :], MG[:, h, :], MS[:, h, :], ALU.mult)
            ins.then_inc(mm["gate_ready"], 1)
            for x in MSEQ:
                kind, t = x
                if kind == "K":
                    layer_wait(dve, l, "turned", TURN[x] + 1)
                    dve.tensor_copy(KTM[:, t % 2, :, P:2 * P], PS[:, 7, :].rearrange("p (h m) -> p h m", h=MH)).then_inc(mm["low_copied"], 1)
                elif kind == "P":
                    layer_wait(dve, l, "scores", t + 1)
                    a = 4 - 2 * (t % 2)
                    mine(dve.tensor_reduce(sm[:, t % 2, 0, :], PS[:, a:a + 2, :].rearrange("p b (h m) -> p (b h) m", h=2), AX.X, ALU.max))
                    mine.wait()
                    dve.tensor_scalar(sm[:, t % 2, 1, :], sm[:, t % 2, 0, :], -SCALE, None, ALU.mult).then_inc(mm["negmax"], 1)
                    layer_wait(dve, l, "exps", t + 1)
                    mine(dve.reciprocal(sm[:, t % 2, 3, :], sm[:, t % 2, 2, :]))
                    mine.wait()
                    dve.tensor_tensor(PR[:], PR[:], sm[:, t % 2, 3, :].unsqueeze(2).broadcast_to([P, MH, NM]), ALU.mult).then_inc(mm["probs"], 1)
                    layer_wait(dve, l, "turned", TURN[x] + 1)
                    if t:
                        layer_wait(dve, l, "values", t)
                    dve.tensor_copy(PT[:, 1, :, :], PS[:, 7, :].rearrange("p (h m) -> p h m", h=MH)).then_inc(mm["low_copied"], 1)
                elif kind == "A":
                    if t < NT - 1:
                        layer_wait(dve, l, "values", t + 1)
                    else:
                        layer_wait(dve, l, "value_stream", NB)
                    if t == 0:
                        layer_wait(dve, l, "gate_ready", 1)
                    o = PS[:, t % 2, :].rearrange("p (h m) -> p h m", h=MH)
                    c = slice(P * t, P * t + P)
                    dve.tensor_tensor(MQ[:, :, c], o, MS[:, :, c], ALU.mult).then_inc(mm["gated"], 1)

        def mem_pool(pool, l):
            pool.dma_start(MRAW if l == 0 else MQ[:], scr[SRC[l]][2 * MIXB:2 * MIXB + MH].rearrange("k p n -> p k n")).then_inc(mm["q_loaded"], 16)
            pool.dma_start(MG[:], scr[SRC[l]][2 * MIXB + MH:2 * MIXB + 2 * MH].rearrange("k p n -> p k n")).then_inc(mm["g_loaded"], 16)
            for n in range(2 * NB + 1):
                if n == 0:
                    src = out["mem_k_prompt"][l, 0]
                elif n <= NB:
                    src = io["cache_mem_k"][l, n - 1]
                else:
                    src = io["cache_mem_v"][l, n - NB - 1]
                if n >= 3:
                    if n - 3 <= NB:
                        layer_wait(pool, l, "turned", TURN[("K", n - 3)] + 1)
                    else:
                        layer_wait(pool, l, "value_stream", n - 3 - NB)
                pool.dma_start(KVR[:, n % 3], src.rearrange("(t p) h d -> p t (h d)", p=P)).then_inc(mm[f"rows{n % 3}"], 16)
                if n == 0:
                    pool.dma_start(KVR[:, 3], out["mem_v_prompt"][l, 0].rearrange("(t p) h d -> p t (h d)", p=P)).then_inc(mm["vp"], 16)
            layer_wait(pool, l, "gated", NT)
            pool.dma_start(scr[DST[l]][MIXB:KT].rearrange("k p n -> p k n"), MQ[:]).then_inc(mm["stored"], 16)

        s_fld = [sem(f"fill_loaded{k}") for k in range(2)]
        s_fh, s_fl, s_gel = sem("fill_high"), sem("fill_low"), sem("gelu_done")
        s_gt, s_gs, s_gm = [sem(f"gate_loaded{k}") for k in range(2)], sem("gate_sigmoid"), sem("gate_multiplied")
        SG, GT, GS, AO = place([(2, TOK), (2, TOK), (2, TOK), (2, TOK)], at=2 * D)
        F_Y, F_A, F_B = 0, MIXB, MIXB + KT
        s_aost = [sem(f"a_stored{k}") for k in range(2)]

        def fill_pool(pool, first, blocks, src, gate=None):
            for k in range(blocks):
                f = first + k
                if f >= 2:
                    pool.wait_ge(s_fl, f - 1)
                pool.dma_start(EST[:, f % 2, :], src(k)).then_inc(s_fld[f % 2], 16)
                if gate is not None and k < MIXB:
                    if k >= 2:
                        pool.wait_ge(s_gm, MIXB + k - 1)
                    g = MIXB + k
                    pool.dma_start(GT[:, k % 2, :], gate(k)).then_inc(s_gt[k % 2], 16 * 1)

        def fill_act(act, first, blocks, kind):
            for k in range(blocks):
                f = first + k
                act.wait_ge(s_fld[f % 2], 16 * (f // 2 + 1))
                if kind == "gelu":
                    act.activation(EST[:, f % 2, :], EST[:, f % 2, :], ACT.Gelu_apprx_tanh).then_inc(s_gel, 1)
                    act.wait_ge(s_gel, k + 1)
                if kind == "gate" and k < MIXB:
                    act.wait_ge(s_gt[k % 2], 16 * (MIXB // 2 + k // 2 + 1))
                    act.activation(GS[:, k % 2, :], GT[:, k % 2, :], ACT.Sigmoid).then_inc(s_gs, 1)
                    act.wait_ge(s_gm, MIXB + k + 1)
                xh, e = XH[:, k, :], EST[:, f % 2, :]
                if first == F_A and k < MIXB:
                    xh, e = natural(xh), by_step(e)
                act.activation(xh, e, ACT.Copy).then_inc(s_fh, 1)

        def fill_dve(dve, first, blocks, kind):
            for k in range(blocks):
                f = first + k
                if kind == "gate" and k < MIXB:
                    dve.wait_ge(s_gs, MIXB + k + 1)
                    s_tmp = GS[:, k % 2, :]
                    fill_dve.mine(dve.tensor_tensor(s_tmp, s_tmp, GT[:, k % 2, :], ALU.mult))
                    fill_dve.mine.wait()
                    dve.tensor_tensor(EST[:, f % 2, :], EST[:, f % 2, :], s_tmp, ALU.mult).then_inc(s_gm, 1)
                dve.wait_ge(s_fh, f + 1)
                xh, xl, e = XH[:, k, :], XL[:, k, :], EST[:, f % 2, :]
                if first == F_A and k < MIXB:
                    xh, xl, e = natural(xh), natural(xl), by_step(e)
                dve.tensor_tensor(xl, e, xh.bitcast(F32), ALU.subtract).then_inc(s_fl, 1)

        s_osq = [sem(f"out_squared{l}") for l in range(2)]
        s_osum, s_x1, s_x1st = sem("out_summed"), sem("residual_ready"), sem("x1_stored")
        s_gb = sem("g_post_loaded")
        KVS, = place([(NT, RW)])
        s_kvst = [sem(f"kv_stored{t}") for t in range(NT)]

        KR, VR, KTB, QR, QT, TP, SP_, WT, SUM1, SUM0, OS = place(
            [(13, P), (13, P), (13, P), (TOK,), (TOK,), (3, 512), (3, 512), (3, 512), (2 * P,), (3 * P,), (TOK,)])
        s_q, s_qt, s_kr, s_vr = sem("q_rows"), sem("q_scaled"), sem("k_rows"), sem("v_rows")
        s_kt, s_kte, s_z, s_t = sem("k_turned"), sem("k_copied"), sem("z_ready"), sem("softplus_tail")
        s_sp, s_spm, s_sum, s_e = sem("softplus_ready"), sem("softplus_masked"), sem("later_sums"), sem("exponent_ready")
        s_w, s_wm, s_o, s_oe, s_ost = sem("weights_exp"), sem("weights_masked"), sem("head_product"), sem("head_copied"), sem("head_stored")

        DIAG = [(0, 0), (1, 0), (2, 0), (2, 2 * P)]
        NEW, PASTC = (1, 3 * P), (2, 3 * P)

        def sb_pe(pe, i, r):
            h = i * 2 + r

            def turn():
                pe.wait_ge(s_kr, h * 48 + 48)
                pe.wait_ge(s_oe, h * 2 + 2)
                for x in range(4):
                    for j in range(4 * x, min(4 * x + 4, 13)):
                        ins = pe.transpose(PS[:, 4 + x, (j % 4) * P:(j % 4 + 1) * P], KR[:, j, :], ident[:])
                    ins.then_inc(s_kt, 1)

            def scores():
                pe.wait_ge(s_kte, h * 4 + 4)
                pe.wait_ge(s_qt, h + 2)
                pe.matmul(PS[:, 4, :], KTB[:, 0, :], QT[:, 0:SEQ], start=True, stop=False, skip_group_check=True)
                pe.matmul(PS[:, 5, 0:3 * P], KTB[:, 1, :], QT[:, P:SEQ], start=True, stop=False, skip_group_check=True)
                pe.matmul(PS[:, 5, 3 * P:], KTB[:, 4, :], QT[:, SEQ:TOK], start=False, stop=False, skip_group_check=True)
                pe.matmul(PS[:, 6, 0:2 * P], KTB[:, 2, :], QT[:, 2 * P:SEQ], start=True, stop=False, skip_group_check=True)
                pe.matmul(PS[:, 6, 2 * P:3 * P], KTB[:, 3, :], QT[:, 3 * P:SEQ], start=False, stop=False, skip_group_check=True)
                for b in range(NB):
                    ins = pe.matmul(PS[:, 6, 3 * P + DSEQ * b:3 * P + DSEQ * (b + 1)], KTB[:, 5 + b, :],
                                    QT[:, SEQ + DSEQ * b:SEQ + DSEQ * (b + 1)], start=False, stop=False, skip_group_check=True)
                ins.then_inc(s_z, 1)

            def exponents():
                pe.wait_ge(s_spm, h + 1)
                pe.wait_ge(s_sum, h + 1)
                pe.wait_ge(s_t, h + 1)
                kw = dict(start=False, stop=False, skip_group_check=True)
                pe.matmul(PS[:, 4, P:], ones[:], SUM0[:], **kw)
                pe.matmul(PS[:, 5, P:3 * P], ones[:], SUM1[:], **kw)
                pe.matmul(PS[:, 6, P:2 * P], ones[:], SP_[:, 2, 2 * P:3 * P], **kw)
                pe.matmul(PS[:, 6, 3 * P:], ones[:], SP_[:, 1, 3 * P:], **kw)
                for x in range(3):
                    ins = pe.matmul(PS[:, 4 + x, :], tri[:], SP_[:, x, :], start=False, stop=True, skip_group_check=True)
                    ins.then_inc(s_e, 1)

            def values():
                pe.wait_ge(s_wm, h + 1)
                pe.wait_ge(s_w, h * 3 + 3)
                pe.wait_ge(s_vr, h * 48 + 48)
                kw = dict(skip_group_check=True)
                pe.matmul(PS[:, 7, :], VR[:, 0, :], WT[:, 0, :], start=True, stop=False, **kw)
                pe.matmul(PS[:, 7, P:], VR[:, 1, :], WT[:, 1, 0:3 * P], start=False, stop=False, **kw)
                pe.matmul(PS[:, 7, 2 * P:], VR[:, 2, :], WT[:, 2, 0:2 * P], start=False, stop=False, **kw)
                pe.matmul(PS[:, 7, 3 * P:], VR[:, 3, :], WT[:, 2, 2 * P:3 * P], start=False, stop=True, **kw).then_inc(s_o, 1)
                pe.matmul(PS[:, 4, 0:P], VR[:, 4, :], WT[:, 1, 3 * P:], start=True, stop=False, **kw)
                for b in range(NB):
                    c = slice(DSEQ * b, DSEQ * (b + 1))
                    ins = pe.matmul(PS[:, 4, c], VR[:, 5 + b, :], WT[:, 2, 3 * P + DSEQ * b:3 * P + DSEQ * (b + 1)],
                                    start=False, stop=True, **kw)
                ins.then_inc(s_o, 1)

            return turn, scores, exponents, values

        def loop_wait(pool, s, count):
            count = pool.snap(pool.to_reg(count))
            pool.wait_ge(s_memset, 1)
            pool.wait_ge(s, count)

        def sb_pool(pool, mine, i):
            for r in range(2):
                h = i * 2 + r
                loop_wait(pool, s_kt, h * 4 + 4)
                for name, dst, s in (("k", KR, s_kr), ("v", VR, s_vr)):
                    if name == "v":
                        loop_wait(pool, s_o, h * 2 + 2)
                    hd = (slice(None), slice(None), ds(h, 1))
                    a = out[f"{name}_prompt"][0].rearrange("(t p) h d -> h p t d", p=P)[ds(h, 1)].rearrange("o p t d -> (o p) t d")
                    pool.dma_start(dst[:, 0:4, :], a).then_inc(s, 16)
                    a = out[f"{name}_sample"].rearrange("b i h d -> h (b i) d")[ds(h, 1)].rearrange("o p d -> (o p) d")
                    pool.dma_start(dst[:, 4, :], a).then_inc(s, 16)
                    a = io[f"cache_{name}"].rearrange("b p h d -> h p b d")[ds(h, 1)].rearrange("o p b d -> (o p) b d")
                    pool.dma_start(dst[:, 5:13, :], a).then_inc(s, 16)
                for src, ready, done in ((SP_, s_sp, s_spm), (WT, s_w, s_wm)):
                    loop_wait(pool, ready, h * 3 + 3)
                    for x, c in DIAG + [NEW]:
                        v = src[:, x, c:c + P]
                        ins = pool.affine_select(out=v, in_=v, compare_op=ALU.is_gt, fill=0.0, base=0, pattern=[[1, P]], channel_multiplier=-1)
                    mine(ins)
                    loop_wait(pool, mine.sem, mine.count())
                    v = src[:, NEW[0], NEW[1]:NEW[1] + P].rearrange("p (b i) -> p b i", b=NB)
                    pool.affine_select(out=v, in_=v, compare_op=ALU.is_ge, fill=0.0, base=0,
                                       pattern=[[-DSEQ, NB], [0, DSEQ]], channel_multiplier=1).then_inc(done, 1)

        def sb_act(act, i, r):
            h = i * 2 + r

            def turn():
                for m in range(2):
                    act.wait_ge(s_st["in_b"][m], i * 32 + 16)
                act.wait_ge(s_qt, h + 1)
                act.dma_start(QR[:], scr["in_b"][ds(h, 1)].rearrange("o p n -> (o p) n")).then_inc(s_q, 16)
                act.wait_ge(s_z, h + 1)
                for x in range(4):
                    n = min(4, 13 - 4 * x)
                    act.wait_ge(s_kt, h * 4 + 5 + x)
                    act.activation(KTB[:, 4 * x:4 * x + n, :], PS[:, 4 + x, 0:n * P].rearrange("p (j m) -> p j m", m=P), ACT.Copy).then_inc(s_kte, 1)
                act.wait_ge(s_q, h * 16 + 16)
                act.activation(QT[:], QR[:], ACT.Copy, scale=SCALE).then_inc(s_qt, 1)

            def softplus():
                act.wait_ge(s_z, h + 2)
                act.activation(TP[:], PS[:, 4:7, :], ACT.Abs).then_inc(s_ab, 1)
                act.wait_ge(s_ab, h * 2 + 1)
                act.activation(TP[:], TP[:], ACT.Exp, scale=-1.0).then_inc(s_ab, 1)
                act.wait_ge(s_ab, h * 2 + 2)
                act.activation(TP[:], TP[:], ACT.Ln, bias=1.0).then_inc(s_t, 1)

            def exponential():
                act.wait_ge(s_o, h * 2 + 2)
                for x in range(3):
                    act.wait_ge(s_e, h * 3 + 1 + x)
                    act.activation(WT[:, x, :], PS[:, 4 + x, :], ACT.Exp).then_inc(s_w, 1)

            def output():
                act.wait_ge(s_ost, h * 16 + 16)
                act.wait_ge(s_o, h * 2 + 3)
                act.activation(OS[:, 0:SEQ], PS[:, 7, :], ACT.Copy).then_inc(s_oe, 1)
                act.wait_ge(s_o, h * 2 + 4)
                act.activation(OS[:, SEQ:TOK], PS[:, 4, 0:P], ACT.Copy).then_inc(s_oe, 1)
                act.wait_ge(s_oe, h * 2 + 4)
                act.dma_start(scr["out_b"][ds(h, 1)].rearrange("o p n -> (o p) n"), OS[:]).then_inc(s_ost, 16)

            return turn, softplus, exponential, output

        s_ab = sem("magnitudes")

        def sb_dve(dve, mine, i, r):
            h = i * 2 + r

            def softplus():
                dve.wait_ge(s_t, h + 1)
                for x in range(3):
                    dve.scalar_tensor_tensor(out=SP_[:, x, :], in0=PS[:, 4 + x, :], scalar=0.0, in1=TP[:, x, :],
                                             op0=ALU.max, op1=ALU.add).then_inc(s_sp, 1)
                dve.wait_ge(s_spm, h + 1)
                mine(dve.tensor_copy(SUM1[:, 0:P], SP_[:, 2, 0:P]))
                mine(dve.tensor_tensor(SUM1[:, P:], SP_[:, 2, P:2 * P], SP_[:, 2, 2 * P:3 * P], ALU.add))
                mine(dve.tensor_copy(SUM0[:, 0:P], SP_[:, 1, 0:P]))
                mine.wait()
                dve.tensor_tensor(SUM0[:, P:], SP_[:, 1, P:3 * P], SUM1[:], ALU.add).then_inc(s_sum, 1)

            return softplus

        DVE_SSM, POOL_SSM = 67, 11
        block = ctx.enter_context(nc.Block())

        @block.sync
        def _(sp):
            def src_wide(w, k, kts, c0, cw):
                return w.rearrange("(k p) n -> p k n", p=P)[:, k * kts:(k + 1) * kts, c0:c0 + cw] if isinstance(c0, int) \
                    else w.rearrange("(k p) n -> p k n", p=P)[:, k * kts:(k + 1) * kts, ds(c0, cw)]

            ph = phases["mem"]
            for c in range(4):
                w = (io["w_mem_k"] if c % 2 == 0 else io["w_mem_v"])[c // 2]
                for k in range(ph.upc):
                    load_unit(sp, ph, ph.first + 8 * c + k, k, src_wide(w, k, 2, 0, RW))

            def chunk(ph, n, col):
                for k in range(ph.upc):
                    load_unit(sp, ph, ph.first + ph.upc * n + k, k, src_wide(ph.w, k, ph.kts, col, ph.cw))

            def projections(ph):
                chunk(ph, 0, 0)
                with sp.Fori(0, BATCHES) as i:
                    chunk(ph, 2 * i + 1, i * CW + CW)
                    chunk(ph, 2 * i + 2, i * CW + 7 * CW)
                for n in range(13, 16):
                    chunk(ph, n, n * CW)

            def plain(ph):
                with sp.Fori(0, ph.chunks) as i:
                    chunk(ph, i, i * ph.cw)

            projections(phases["in_a"])
            plain(phases["glu"])
            plain(phases["out_a"])
            plain(phases["kv"])
            projections(phases["in_b"])
            plain(phases["out_b"])
        def unit_stationary(pe, ph, U, k, n):
            pe.wait_ge(s_wl, U + 1)
            pe.wait_ge(s_wh, U + 1)
            wh, wl = wview(WH, k % RING, ph), wview(WL, k % RING, ph)
            for q in range(4):
                m, h = q // 2, q % 2
                if k == 0 and not (isinstance(n, int) and n == 0):
                    pe.wait_ge(s_ev[ph.name], 4 * n - 3 + q)
                for kt in range(ph.kts):
                    last = k == ph.upc - 1 and kt == ph.kts - 1
                    x = (slice(None), k * ph.kts + kt, slice(h * HALF, h * HALF + HALF))
                    w = (slice(None), kt, slice(m * P, m * P + P))
                    ins = three(pe, PS[:, q, 0:HALF], wh[w], wl[w], XH[x], XL[x], k == 0 and kt == 0, last)
                if q == 3:
                    ins.then_inc(s_wu, 1)
                elif k == ph.upc - 1:
                    ins.then_inc(s_bank[ph.name], 1)

        def unit_moving(pe, ph, U, k, n, tiles):
            pe.wait_ge(s_wl, U + 1)
            pe.wait_ge(s_wh, U + 1)
            wh, wl = wview(WH, k % RING, ph), wview(WL, k % RING, ph)
            for t in range(tiles):
                if k == 0 and not (isinstance(n, int) and n == 0):
                    pe.wait_ge(s_ev[ph.name], tiles * n - tiles + 1 + t)
                for kt in range(ph.kts):
                    xh, xl = XH[:, k * ph.kts + kt, P * t:P * t + P], XL[:, k * ph.kts + kt, P * t:P * t + P]
                    first, last = k == 0 and kt == 0, k == ph.upc - 1 and kt == ph.kts - 1
                    pe.matmul(PS[:, t, :], xh, wh[:, kt, :], start=first, stop=False)
                    pe.matmul(PS[:, t, :], xh, wl[:, kt, :], start=False, stop=False)
                    ins = pe.matmul(PS[:, t, :], xl, wh[:, kt, :], start=False, stop=last)
                if t == tiles - 1:
                    ins.then_inc(s_wu, 1)
                elif k == ph.upc - 1:
                    ins.then_inc(s_bank[ph.name], 1)

        def bank_full(eng, ph, n, q, banks):
            if q == banks - 1:
                eng.wait_ge(s_wu, ph.upc * n + ph.first + ph.upc)
            else:
                eng.wait_ge(s_bank[ph.name], (banks - 1) * n + q + 1)

        def turn_rows(pe, r, slot):
            for kg in range(4):
                x = 4 * r + kg
                if x >= 2:
                    pe.wait_ge(s_xl, x - 1)
                for j in range(4):
                    kt = 4 * kg + j
                    ins = pe.transpose(PS[:, 5 + x % 2, j * P:(j + 1) * P], ROW[:, slot, kt * P:(kt + 1) * P], ident[:])
                ins.then_inc(s_xt, 1)

        def turned_view(v, r, kg):
            v = v[:, 4 * kg:4 * kg + 4, :]
            if r < 2:
                return v[:, :, P * r:P * r + P]
            if r < 7:
                return v.rearrange("p k (s c) -> p k s c", s=STEPS)[:, :, :, 16 * (r - 2):16 * (r - 2) + 16]
            return v[:, :, P * (r - 7):P * (r - 7) + P]

        def bank_view(r, x):
            v = PS[:, 5 + x % 2, :].rearrange("p (k m) -> p k m", k=4)
            return v if r < 2 or r >= 7 else v.rearrange("p k (s c) -> p k s c", s=STEPS)

        def turned_high(act, r):
            for kg in range(4):
                x = 4 * r + kg
                act.wait_ge(s_xt, x + 1)
                act.activation(turned_view(XH, r, kg), bank_view(r, x), ACT.Copy).then_inc(s_xh, 1)

        def turned_low(dve, r):
            for kg in range(4):
                x = 4 * r + kg
                dve.wait_ge(s_xh, x + 1)
                dve.tensor_tensor(turned_view(XL, r, kg), bank_view(r, x), turned_view(XH, r, kg).bitcast(F32),
                                  ALU.subtract).then_inc(s_xl, 1)

        def stage_out(act, ph, n, q, banks, stage, first_store, store_sem, width, half=0):
            bank_full(act, ph, n, q, banks)
            act.activation(stage, PS[:, q, 0:width], ACT.Copy).then_inc(s_ev[ph.name], 1)

        def rows_squared(act, src, col, done, junk):
            if done:
                act.wait_ge(s_sq, done)
            act.activation(junk, src, ACT.Square, accum_out=ss[:, col:col + 1]).then_inc(s_sq, 1)

        s_yout = [sem(f"y_row_stored{k}") for k in range(2)]

        def inverse_rms(pool, order, k, summed, count):
            pool.wait_ge(summed, count)
            a = slice(k, k + 1)
            order(pool.tensor_scalar(rstd[:, a], ss[:, a], 1.0 / D, EPS, ALU.mult, ALU.add))
            order.wait()
            pool.tensor_tensor(rstd[:, a], rstd[:, a], nhalf[:, 0:1], ALU.pow).then_inc(s_rs, 1)

        @block.tensor
        def _(pe):
            pe.wait_ge(s_memset, 1)
            pe.wait_ge(s_vecd, 64)
            pe.transpose(PS[:, 7, 0:60], VROW[0:60, :], ident[0:60, 0:60]).then_inc(s_vect, 1)
            for r in range(2):
                pe.wait_ge(s_rowd[r % 2], 16)
                turn_rows(pe, r, r)
            pe.wait_ge(s_par, 64)
            pe.wait_ge(s_parE, 1)
            for j, (src, n) in enumerate(((PRM[0:48, 0, :], 48), (PRM[0:48, 1, :], 48), (PRM[0:48, 2, :], 48), (PRD[0:G, :], G))):
                ins = pe.transpose(PS[:, 7, 64 + 48 * j:64 + 48 * j + n], src, ident[0:n, 0:n])
            ins.then_inc(s_parT, 1)
            ph = phases["mem"]
            pe.wait_ge(s_xl, 8)
            for n in range(4):
                for k in range(ph.upc):
                    unit_moving(pe, ph, ph.first + 8 * n + k, k, n, 2)
            for t in range(NT):
                pe.wait_ge(s_row, t + 1)
                turn_rows(pe, t + 2, t % 2)
            ph = phases["in_a"]
            pe.wait_ge(s_xl, 28)
            pe.wait_ge(s_ev["mem"], 8)

            def chunk(ph, n):
                for k in range(ph.upc):
                    unit_stationary(pe, ph, ph.upc * n + ph.first + k, k, n)

            chunk(ph, 0)
            with pe.Fori(0, BATCHES) as i:
                ssm_pe(pe, ph, i)
            for n in range(13, 16):
                chunk(ph, n)

            pe.wait_ge(s_ev["in_a"], 64)
            pe.wait_ge(s_ye, 21)
            pe.wait_ge(s_fTe, 7)
            mem_pe(pe, 0)
            ph = phases["glu"]
            pe.wait_ge(s_fl, F_Y + MIXB)
            layer_wait(pe, 0, "gated", NT)
            chunk(ph, 0)
            with pe.Fori(1, ph.chunks) as i:
                chunk(ph, i)

            def row_chunks(ph):
                for k in range(ph.upc):
                    unit_moving(pe, ph, ph.first + k, k, 0, NT)
                with pe.Fori(1, ph.chunks) as i:
                    for k in range(ph.upc):
                        unit_moving(pe, ph, ph.upc * i + ph.first + k, k, i, NT)

            pe.wait_ge(s_fl, F_A + KT)
            pe.wait_ge(s_ev["glu"], 24)
            row_chunks(phases["out_a"])
            pe.wait_ge(s_ev["out_a"], 20)
            for t in range(NT):
                pe.wait_ge(s_row, NT + t + 1)
                turn_rows(pe, 7 + t, (7 + t) % 2)
            pe.wait_ge(s_xl, 48)
            row_chunks(phases["kv"])
            pe.wait_ge(s_ev["kv"], 30)
            ph = phases["in_b"]
            chunk(ph, 0)
            with pe.Fori(0, BATCHES) as i:
                first, second = sb_pe(pe, i, 0), sb_pe(pe, i, 1)
                plan = {0: [first[0]], 1: [first[1]], 3: [first[2]], 4: [first[3], second[0]], 5: [second[1]], 7: [second[2]]}
                for x in range(8):
                    for f in plan.get(x, ()):
                        f()
                    n = i * 2 + 1 + x // 4
                    unit_stationary(pe, ph, (i * 2 + 1 + x // 4) * 4 + ph.first + x % 4, x % 4, n)
                second[3]()
            for n in range(13, 16):
                chunk(ph, n)
            pe.wait_ge(s_ev["in_b"], 64)
            pe.wait_ge(s_oe, 26)
            mem_pe(pe, 1)
            pe.wait_ge(s_fl, F_B + KT)
            layer_wait(pe, 1, "gated", NT)
            row_chunks(phases["out_b"])

        @block.scalar
        def _(act):
            mine = Order(act, s_act)
            act.wait_ge(s_vect, 1)
            act.activation(vec[:, 0:60], PS[:, 7, 0:60], ACT.Copy).then_inc(s_vec, 1)
            act.wait_ge(s_vec, 1)
            for U in range(LEAD):
                split_high(act, phases["mem"], U, U)
            for r in range(2):
                turned_high(act, r)
            ph = phases["mem"]
            for n in range(4):
                for k in range(ph.upc):
                    ahead(split_high, act, ph, ph.first + ph.upc * n + k, k)
                for t in range(2):
                    if n:
                        act.wait_ge(s_st["mem"][t], 16 * n)
                    stage_out(act, ph, n, t, 2, EST[:, t, 0:RW], 0, None, RW)
                    act.wait_ge(s_ev["mem"], 2 * n + t + 1)
                    dst = out["mem_k_prompt" if n % 2 == 0 else "mem_v_prompt"][n // 2, 0].rearrange("m h d -> m (h d)")
                    act.dma_start(dst[P * t:P * t + P, :], EST[:, t, 0:RW]).then_inc(s_st["mem"][t], 16)
                if n == 0:
                    for t in range(2):
                        act.wait_ge(s_rowd[t % 2], 32)
                        rows_squared(act, ROW[:, t % 2, :], t, t, JUNK[:])
                    act.wait_ge(s_trig, 1)
                    act.activation(CPT(11), CPT(8), ACT.Sin)
                    act.activation(CPT(12), CPT(10), ACT.Sin).then_inc(s_sin, 1)
            for t in range(NT):
                if t >= 2:
                    act.wait_ge(s_rowd[t % 2], 32 + 16 * (t // 2))
                    rows_squared(act, ROW[:, t % 2, :], t, t, JUNK[:])
                if t >= 1:
                    turned_high(act, t + 1)
            turned_high(act, NT + 1)
            ph = phases["in_a"]

            def store_blocks(name, n, col, q):
                m, h = q // 2, q % 2
                ph = phases[name]
                if h == 0:
                    if not (isinstance(n, int) and n == 0):
                        act.wait_ge(s_st[name][m], n * 16)
                bank_full(act, ph, n, q, 4)
                act.activation(EST[:, m, h * HALF:h * HALF + HALF], PS[:, q, 0:HALF], ACT.Copy).then_inc(s_ev[name], 1)
                if h == 1:
                    act.wait_ge(s_ev[name], n * 4 + q + 1)
                    dst = scr[name][ds(col * 2 + m, 1)].rearrange("o p n -> (o p) n") if not isinstance(col, int) \
                        else scr[name][col * 2 + m]
                    act.dma_start(dst, EST[:, m, :]).then_inc(s_st[name][m], 16)

            def chunk(name, n, col, aux=()):
                ph = phases[name]
                for k in range(ph.upc):
                    ahead(split_high, act, ph, ph.upc * n + ph.first + k, k)
                    if k < len(aux) and aux[k]:
                        aux[k]()
                for q in range(4):
                    store_blocks(name, n, col, q)

            for t in range(2):
                act.wait_ge(s_st["mem"][t], 64)
            chunk("in_a", 0, 0)
            with act.Fori(0, BATCHES) as i:
                aux = ssm_act(act, mine, i)
                chunk("in_a", i * 2 + 1, i + 1, aux[0:4])
                chunk("in_a", i * 2 + 2, i + 7, aux[4:8])
                aux[8]()
            for n in range(13, 16):
                chunk("in_a", n, n)
            act.wait_ge(s_wu, phases["glu"].first)
            fill_act(act, F_Y, MIXB, "gelu")
            mem_act(act, mine, 0)
            ph = phases["glu"]
            for n in range(ph.chunks):
                for k in range(ph.upc):
                    ahead(split_high, act, ph, ph.upc * n + ph.first + k, k)
                    if k < 2:
                        kb = 2 * n + k
                        act.wait_ge(s_gt[k], 16 * (n + 1))
                        if kb >= 2:
                            act.wait_ge(s_gm, kb - 1)
                        act.activation(GS[:, k, :], GT[:, k, :], ACT.Sigmoid).then_inc(s_gs, 1)
                for q in range(4):
                    m, h = q // 2, q % 2
                    bank_full(act, ph, n, q, 4)
                    act.activation(SG[:, m, h * HALF:h * HALF + HALF], PS[:, q, 0:HALF], ACT.Sigmoid,
                                   bias=vec[:, 48 + 2 * n + m:49 + 2 * n + m]).then_inc(s_ev["glu"], 1)
            act.wait_ge(s_wu, phases["out_a"].first)
            fill_act(act, F_A, KT, "plain")

            def out_rows_squared(l):
                ph = phases[DST[l]]
                for n in range(ph.chunks):
                    for k in range(ph.upc):
                        ahead(split_high, act, ph, ph.upc * n + ph.first + k, k)
                    for t in range(NT):
                        bank_full(act, ph, n, t, NT)
                        if n or t:
                            act.wait_ge(s_osq[l], NT * n + t)
                        act.activation(JUNK2[:], PS[:, t, :], ACT.Square, accum_out=ss4[:, l, t, n:n + 1]).then_inc(s_osq[l], 1)

            out_rows_squared(0)

            def x1_squared(t):
                act.wait_ge(s_x1, t + 1)
                rows_squared(act, OUTROW[:, t, :], 10 + t, NT + t, ROW[:, (7 + t) % 2, :])

            x1_squared(0)
            x1_squared(1)
            for t in range(NT):
                turned_high(act, 7 + t)
                if t + 2 < NT:
                    x1_squared(t + 2)
            ph = phases["kv"]

            def kv_chunk(n, name, col):
                for k in range(ph.upc):
                    ahead(split_high, act, ph, ph.upc * n + ph.first + k, k)
                for t in range(NT):
                    if not (isinstance(n, int) and n == 0):
                        act.wait_ge(s_kvst[t], n * 16)
                    bank_full(act, ph, n, t, NT)
                    act.activation(KVS[:, t, :], PS[:, t, :], ACT.Copy).then_inc(s_ev["kv"], 1)
                for t in range(NT):
                    act.wait_ge(s_ev["kv"], n * NT + t + 1)
                    dst = out[f"{name}_prompt"][0].rearrange("l h d -> l (h d)")[P * t:P * t + P] if t < NT - 1 else \
                        out[f"{name}_sample"].rearrange("b i h d -> (b i) (h d)")
                    act.dma_start(dst[:, ds(col, RW)], KVS[:, t, :]).then_inc(s_kvst[t], 16)

            kv_chunk(0, "k", 0)
            with act.Fori(1, 3) as i:
                kv_chunk(i, "k", i * RW)
            with act.Fori(3, 5) as i:
                kv_chunk(i, "v", i * RW - 3 * RW)
            kv_chunk(5, "v", 2 * RW)
            chunk("in_b", 0, 0)
            with act.Fori(0, BATCHES) as i:
                first, second = sb_act(act, i, 0), sb_act(act, i, 1)

                def between():
                    first[3]()
                    second[0]()

                chunk("in_b", i * 2 + 1, i + 1, [first[0], first[1], None, first[2]])
                chunk("in_b", i * 2 + 2, i + 7, [between, second[1], None, second[2]])
                second[3]()
            for n in range(13, 16):
                chunk("in_b", n, n)
            mem_act(act, mine, 1)
            act.wait_ge(s_wu, phases["out_b"].first)
            fill_act(act, F_B, KT, "gate")
            out_rows_squared(1)

        @block.vector
        def _(dve):
            mine = Order(dve, s_dve)
            dve.wait_ge(s_vec, 1)
            ssm_params(dve, mine)
            for U in range(LEAD):
                split_low(dve, phases["mem"], U, U)
            for r in range(2):
                turned_low(dve, r)
            ssm_params2(dve, mine)
            ph = phases["mem"]
            for n in range(4):
                for k in range(ph.upc):
                    ahead(split_low, dve, ph, ph.first + ph.upc * n + k, k)
                if n == 0:
                    ssm_params3(dve, mine)
            for t in range(NT):
                dve.wait_ge(s_rs, t + 1)
                dve.tensor_scalar(ROW[:, t % 2, :], ROW[:, t % 2, :], rstd[:, t:t + 1], None, ALU.mult).then_inc(s_row, 1)
                if t >= 1:
                    turned_low(dve, t + 1)
            turned_low(dve, NT + 1)

            def chunk(ph, n, aux=()):
                for k in range(ph.upc):
                    ahead(split_low, dve, ph, ph.upc * n + ph.first + k, k)
                    if k < len(aux) and aux[k]:
                        aux[k]()

            ph = phases["in_a"]
            chunk(ph, 0)
            with dve.Fori(0, BATCHES) as i:
                mine.enter(i, DVE_SSM)
                aux = ssm_dve(dve, mine, i)
                chunk(ph, i * 2 + 1, aux[0:4])
                chunk(ph, i * 2 + 2, aux[4:8])
                aux[8]()
                mine.leave(BATCHES)
            for n in range(13, 16):
                chunk(ph, n)
            fill_dve.mine = mine
            fill_dve(dve, F_Y, MIXB, "gelu")
            mem_dve(dve, mine, 0)
            ph = phases["glu"]
            for n in range(ph.chunks):
                for k in range(ph.upc):
                    ahead(split_low, dve, ph, ph.upc * n + ph.first + k, k)
                for m in range(2):
                    kb = 2 * n + m
                    if n:
                        dve.wait_ge(s_aost[m], 16 * n)
                    dve.wait_ge(s_gs, kb + 1)
                    mine(dve.tensor_tensor(AO[:, m, :], XH[:, kb, :].bitcast(F32), XL[:, kb, :].bitcast(F32), ALU.add))
                    mine(dve.tensor_tensor(GS[:, m, :], GS[:, m, :], GT[:, m, :], ALU.mult))
                    mine.wait()
                    mine(dve.tensor_tensor(AO[:, m, :], AO[:, m, :], GS[:, m, :], ALU.mult))
                    mine.wait()
                    dve.wait_ge(s_ev["glu"], 4 * n + 2 * m + 2)
                    dve.tensor_tensor(AO[:, m, :], AO[:, m, :], SG[:, m, :], ALU.mult).then_inc(s_gm, 1)
            fill_dve(dve, F_A, KT, "plain")

            def out_rows(l):
                ph = phases[DST[l]]
                for n in range(ph.chunks):
                    for k in range(ph.upc):
                        ahead(split_low, dve, ph, ph.upc * n + ph.first + k, k)
                    if n == 0:
                        dve.wait_ge(s_gb, 16 * (l + 1))
                    for t in range(NT):
                        dve.wait_ge(s_osq[l], NT * n + t + 1)
                        c = slice(n * RW, n * RW + RW)
                        dve.tensor_tensor(OUTROW[:, t, c], PS[:, t, :], GB[:, c], ALU.mult).then_inc(s_ev[ph.name], 1)
                for t in range(NT):
                    k = 5 + 10 * l + t
                    dve.tensor_reduce(ss[:, k:k + 1], ss4[:, l, t, :], AX.X, ALU.add).then_inc(s_osum, 1)

            def residual(l, t):
                r = 7 + 5 * l + t
                dve.wait_ge(s_rs, 5 + 10 * l + t + 1)
                dve.wait_ge(s_rowd[r % 2], 16 * (r // 2 + 1))
                dve.wait_ge(s_ev[DST[l]], 20)
                k = 5 + 10 * l + t
                dst = OUTROW[:, t, :] if l == 0 else ROW[:, r % 2, :]
                dve.scalar_tensor_tensor(out=dst, in0=OUTROW[:, t, :], scalar=rstd[:, k:k + 1], in1=ROW[:, r % 2, :],
                                         op0=ALU.mult, op1=ALU.add).then_inc(s_x1, 1)

            out_rows(0)
            residual(0, 0)
            residual(0, 1)
            for t in range(NT):
                dve.wait_ge(s_rs, 10 + t + 1)
                dve.tensor_scalar(ROW[:, (7 + t) % 2, :], OUTROW[:, t, :], rstd[:, 10 + t:11 + t], None, ALU.mult).then_inc(s_row, 1)
                turned_low(dve, 7 + t)
                if t + 2 < NT:
                    residual(0, t + 2)
            ph = phases["kv"]
            with dve.Fori(0, 5) as i:
                chunk(ph, i)
            chunk(ph, 5)
            ph = phases["in_b"]
            chunk(ph, 0)
            with dve.Fori(0, BATCHES) as i:
                mine.enter(i, 6)
                chunk(ph, i * 2 + 1, [None, sb_dve(dve, mine, i, 0)])
                chunk(ph, i * 2 + 2, [None, sb_dve(dve, mine, i, 1)])
                mine.leave(BATCHES)
            for n in range(13, 16):
                chunk(ph, n)
            mem_dve(dve, mine, 1)
            fill_dve(dve, F_B, KT, "gate")
            out_rows(1)
            for t in range(NT):
                residual(1, t)

        @block.gpsimd
        def _(pool):
            mine = Order(pool, s_pool)
            mine(pool.memset(ident[:], 0.0))
            mine(pool.memset(nhalf[:], -0.5))
            mine(pool.memset(tri[:], -1.0))
            mine(pool.memset(ones[:], -1.0))
            mine.wait()
            mine(pool.affine_select(out=ident[:], in_=ident[:], compare_op=ALU.not_equal, fill=1.0, base=0,
                                    pattern=[[-1, P]], channel_multiplier=1))
            mine(pool.affine_select(out=tri[:], in_=tri[:], compare_op=ALU.is_ge, fill=0.0, base=0,
                                    pattern=[[-1, P]], channel_multiplier=1))
            mine.wait()
            pool.memset(marks[0:1, 0:1], 0.0).then_inc(s_memset, 1)
            for a, b, name in ((0, 16, "g_pre_a"), (16, 32, "g_kv"), (32, 48, "g_pre_b"), (48, 60, "b_glu")):
                v = io[name] if name == "g_kv" else io[name][0]
                pool.dma_start(VROW[a:b, :], v.rearrange("(k p) -> k p", p=P)).then_inc(s_vecd, 16)
            for r in range(2):
                pool.dma_start(ROW[:, r, :], io["mem_prompt"][0, P * r:P * r + P, :]).then_inc(s_rowd[r], 16)
            for j, name in enumerate(("ssm_lam_re", "ssm_lam_im")):
                pool.dma_start(PRM[0:48, j, :], io[name][0].rearrange("(j q) p -> j (q p)", q=2)).then_inc(s_par, 16)
            pool.dma_start(PRL[0:48, :], io["ssm_log_dt"][0].rearrange("(j q) -> j q", q=2)).then_inc(s_par, 16)
            pool.dma_start(DRW[0:G, :], io["ssm_d"][0]).then_inc(s_par, 16)
            pool.memset(TZ[:], 0.0).then_inc(s_zero, 1)
            pool.memset(HPZ[:], 0.0).then_inc(s_zero, 1)
            pool.memset(BB[:], 0.0).then_inc(s_zero, 1)
            prime_ssm(pool)
            for k, (s, n) in enumerate(((s_oe, 2), (s_kt, 4), (s_qt, 1), (s_z, 1), (s_o, 2), (s_ost, 16))):
                pool.memset(marks[0:1, 20 + k:21 + k], 0.0).then_inc(s, n)
            for t in range(NT):
                pool.wait_ge(s_xt, 4 * (t + 1))
                pool.dma_start(ROW[:, t % 2, :], x_rows(t)).then_inc(s_rowd[t % 2], 16)
                if t == 1:
                    ssm_params_pool(pool, mine)
                    for u in range(2):
                        inverse_rms(pool, mine, u, s_sq, u + 1)
                if t >= 2:
                    inverse_rms(pool, mine, t, s_sq, t + 1)
            pool.wait_ge(s_xt, 4 * (NT + 2))
            with pool.Fori(0, BATCHES) as i:
                mine.enter(i, POOL_SSM)
                ssm_pool(pool, mine, i)
                mine.leave(BATCHES)
            for m in range(2):
                pool.wait_ge(s_st["in_a"][m], 256)
            pool.wait_ge(s_yst, 896)
            pool.wait_ge(s_fst, 224)
            fill_pool(pool, F_Y, MIXB, lambda k: scr["y"].rearrange("(k g) h n -> k (g h) n", k=MIXB)[k])
            mem_pool(pool, 0)
            layer_wait(pool, 0, "stored", 16)
            for kb in range(2):
                pool.dma_start(GT[:, kb, :], scr["in_a"][MIXB + kb]).then_inc(s_gt[kb], 16)
            for kb in range(MIXB):
                pool.wait_ge(s_gm, kb + 1)
                pool.dma_start(scr["out_a"][kb], AO[:, kb % 2, :]).then_inc(s_aost[kb % 2], 16)
                if kb + 2 < MIXB:
                    pool.dma_start(GT[:, kb % 2, :], scr["in_a"][MIXB + kb + 2]).then_inc(s_gt[kb % 2], 16)
            for m in range(2):
                pool.wait_ge(s_aost[m], 96)
            fill_pool(pool, F_A, KT, lambda k: scr["out_a"][k])
            pool.dma_start(GB[:], io["g_post_a"].broadcast_to([P, D])).then_inc(s_gb, 16)
            for t in range(2):
                pool.dma_start(ROW[:, (7 + t) % 2, :], x_rows_plain(t)).then_inc(s_rowd[(7 + t) % 2], 16)
            for t in range(NT):
                inverse_rms(pool, mine, 5 + t, s_osum, t + 1)
            for t in range(NT):
                pool.wait_ge(s_x1, t + 1)
                pool.dma_start(scr["x1"][P * t:P * t + P, :], OUTROW[:, t, :]).then_inc(s_x1st, 16)
                inverse_rms(pool, mine, 10 + t, s_sq, NT + t + 1)
                if t + 2 < NT:
                    pool.wait_ge(s_xt, 4 * (8 + t))
                    pool.dma_start(ROW[:, (7 + t) % 2, :], x_rows_plain(t + 2)).then_inc(s_rowd[(7 + t) % 2], 16)
            pool.wait_ge(s_x1st, 80)
            for t in range(NT):
                pool.wait_ge(s_kvst[t], 96)
            with pool.Fori(0, BATCHES) as i:
                mine.enter(i, 4)
                sb_pool(pool, mine, i)
                mine.leave(BATCHES)
            for m in range(2):
                pool.wait_ge(s_st["in_b"][m], 256)
            pool.wait_ge(s_ost, 16 * 13)
            mem_pool(pool, 1)
            layer_wait(pool, 1, "stored", 16)
            fill_pool(pool, F_B, KT, lambda k: scr["out_b"][k], lambda k: scr["in_b"][MIXB + k])
            pool.dma_start(GB[:], io["g_post_b"].broadcast_to([P, D])).then_inc(s_gb, 16)
            for t in range(2):
                r = 12 + t
                pool.dma_start(ROW[:, r % 2, :], scr["x1"][P * t:P * t + P, :]).then_inc(s_rowd[r % 2], 16)
            for t in range(NT):
                inverse_rms(pool, mine, 15 + t, s_osum, NT + t + 1)
            for t in range(NT):
                r = 12 + t
                pool.wait_ge(s_x1, NT + t + 1)
                dst = out["y_prompt"][0, P * t:P * t + P, :] if t < NT - 1 else out["y_sample"].rearrange("b i d -> (b i) d")
                pool.dma_start(dst, ROW[:, r % 2, :]).then_inc(s_yout[r % 2], 16)
                if t + 2 < NT:
                    pool.wait_ge(s_yout[r % 2], 16 * (t // 2 + 1))
                    pool.dma_start(ROW[:, r % 2, :], scr["x1"][P * (t + 2):P * (t + 3), :]).then_inc(s_rowd[r % 2], 16)
            pool.wait_ge(s_yout[0], 48)
            pool.wait_ge(s_yout[1], 32)


_OUTS = [("y_prompt", (1, SEQ, D)), ("y_sample", (NB, DSEQ, D)), ("k_prompt", (1, SEQ, HEADS, P)), ("v_prompt", (1, SEQ, HEADS, P)),
         ("k_sample", (NB, DSEQ, HEADS, P)), ("v_sample", (NB, DSEQ, HEADS, P)), ("ssm_prompt", (1, 1, G, ST, 2)),
         ("ssm_sample", (1, NB, G, ST, 2)), ("mem_k_prompt", (2, 1, NM, MH, P)), ("mem_v_prompt", (2, 1, NM, MH, P))]
_SCRATCH = [("in_a", (NBLK, P, TOK)), ("in_b", (NBLK, P, TOK)), ("y", (G, GH, TOK)), ("lags", (G, GH, P)),
            ("out_a", (KT, P, TOK)), ("out_b", (KT, P, TOK)), ("x1", (TOK, D))]


def kernel(**inputs):
    import numpy as _np
    import concourse.bacc as _bacc
    from concourse import mybir as _mybir
    from concourse.bass_utils import run_bass_kernel_spmd as _run

    nc = _bacc.Bacc("TRN2", target_bir_lowering=False, num_devices=1)
    arrays, io = {}, {}
    for name in inputs:
        a = _np.ascontiguousarray(inputs[name])
        arrays[f"in_{name}_dram"] = a
        io[name] = nc.dram_tensor(f"in_{name}_dram", a.shape, _mybir.dt.from_np(a.dtype), kind="ExternalInput").ap()
    out = {name: nc.dram_tensor(f"out_{name}", shape, F32, kind="ExternalOutput").ap() for name, shape in _OUTS}
    scr = {name: nc.dram_tensor(f"scratch_{name}", shape, F32, kind="Internal").ap() for name, shape in _SCRATCH}
    build(nc, io, out, scr)
    r = _run(nc, [arrays], core_ids=[0])
    return tuple(r.results[0][f"out_{name}"] for name, _ in _OUTS)
```

```python
from contextlib import ExitStack
import math

import concourse.bass as bass
from concourse import mybir

F32 = mybir.dt.float32
F32R = mybir.dt.float32r
I32 = mybir.dt.int32
ALU = mybir.AluOpType
ACT = mybir.ActivationFunctionType
AX = mybir.AxisListType
ds = bass.ds

P = 128
D = 2048
KT = D // P
SEQ, NB, DSEQ = 512, 8, 16
NT = SEQ // P + 1
TOK = NT * P
HALF = TOK // 2
MIX, MEMW = 1536, 512
MIXB = MIX // P
NBLK = (2 * MIX + 2 * MEMW) // P
MH, NM = 4, 256
HEADS = MIX // P
EPS = 1e-6
SCALE = 1.0 / math.sqrt(P)
G, ST, GH = 96, 64, 16
PAIRS = G // 2
STEPS = 8
NC = TOK // STEPS
PC = SEQ // STEPS
JB = 8
BATCHES = PAIRS // JB
CW = 256
RW = 512
LEAD = 3
RING = 4
NPW = 23


class Order:

    def __init__(self, eng, sem):
        self.eng, self.sem, self.n, self.start = eng, sem, 0, None

    def __call__(self, ins):
        ins.then_inc(self.sem, 1)
        self.n += 1
        return ins

    def count(self):
        return self.n if self.start is None else self.start[1] * self.start[2] + self.n

    def wait(self):
        self.eng.wait_ge(self.sem, self.count())

    def enter(self, i, per):
        self.start = (self.n, i, per)

    def leave(self, times):
        base, i, per = self.start
        assert self.n - base == per, (self.n - base, per)
        self.n = base + per * times
        self.start = None


def build(nc, io, out, scr):
    with ExitStack() as ctx:
        def sb(name, shape, dt=F32):
            return ctx.enter_context(nc.sbuf_tensor(name, shape, dt))

        def sem(name):
            return ctx.enter_context(nc.semaphore(name))

        ctx.enter_context(nc.allow_non_contiguous_dma(reason="small tables and states"))
        XH, XL = sb("XH", [P, KT, TOK], F32R), sb("XL", [P, KT, TOK], F32R)
        RAW = sb("RAW", [P, 2, 1024])
        WH, WL = sb("WH", [P, RING, 1024], F32R), sb("WL", [P, RING, 1024], F32R)
        EST = sb("EST", [P, 2, TOK])
        ident, tri, ones = sb("ident", [P, P]), sb("tri", [P, P]), sb("ones", [P, P])
        vec = sb("vec", [P, 64])
        ss, rstd, nhalf = sb("ss", [P, 32]), sb("rstd", [P, 32]), sb("nhalf", [P, NT])
        marks = sb("marks", [1, 40])
        FN = 20640
        FA = sb("FA", [P, FN])
        PS = ctx.enter_context(nc.psum_tensor("PS", [P, 8, 512], F32))

        def place(shapes, at=0):
            views = []
            for shape in shapes:
                n = int(math.prod(shape))
                v = FA[:, at:at + n]
                names = "abcde"[:len(shape)]
                if len(shape) > 1:
                    v = v.rearrange("p (" + " ".join(names) + ") -> p " + " ".join(names),
                                    **{names[k]: shape[k] for k in range(len(shape))})
                views.append(v)
                at += n
            assert at <= FN, at
            return views

        class Phase:
            def __init__(self, name, w, units, kts, cw, gcol, first):
                self.name, self.w, self.kts, self.cw, self.gcol, self.first = name, w, kts, cw, gcol, first
                self.upc = units

        phases = {}
        at = 0
        for name, w, kts, cw, gcol, chunks, upc in (
                ("mem", None, 2, RW, None, 4, 8),
                ("in_a", io["w_in_a"][0], 4, CW, 0, 16, 4),
                ("glu", io["w_glu"][0], 3, CW, None, 6, 4),
                ("out_a", io["w_out_a"][0], 2, RW, None, 4, 8),
                ("kv", io["w_kv"], 2, RW, 16, 6, 8),
                ("in_b", io["w_in_b"][0], 4, CW, 32, 16, 4),
                ("out_b", io["w_out_b"][0], 2, RW, None, 4, 8)):
            phases[name] = Phase(name, w, upc, kts, cw, gcol, at)
            phases[name].chunks = chunks
            at += chunks * upc
        UNITS = at
        TABLE = []
        for ph in phases.values():
            TABLE += [(ph, k) for c in range(ph.chunks) for k in range(ph.upc)]

        def wview(t, slot, ph):
            return t[:, slot, 0:ph.kts * ph.cw].rearrange("p (k c) -> p k c", k=ph.kts)

        s_ld = [sem(f"weights_loaded{k}") for k in range(2)]
        s_wh, s_wl, s_wu = sem("weights_high"), sem("weights_low"), sem("weights_used")

        def load_unit(eng, ph, U, k, src):
            par = k % 2
            if not (isinstance(U, int) and U < 2):
                eng.wait_ge(s_wl, U - 1)
                eng.wait_ge(s_wh, U - 1)
            eng.dma_start(wview(RAW, par, ph), src).then_inc(s_ld[par], 16)

        def split_high(eng, ph, U, k):
            par, slot = k % 2, k % RING
            eng.wait_ge(s_ld[par], (U - par) * 8 + 16)
            if not (isinstance(U, int) and U < RING):
                eng.wait_ge(s_wu, U - RING + 1)
            if ph.gcol is None:
                n = ph.kts * ph.cw
                eng.activation(WH[:, slot, 0:n], RAW[:, par, 0:n], ACT.Copy).then_inc(s_wh, 1)
            else:
                for kt in range(ph.kts):
                    g = ph.gcol + (k % ph.upc) * ph.kts + kt
                    ins = eng.activation(wview(WH, slot, ph)[:, kt, :], wview(RAW, par, ph)[:, kt, :], ACT.Copy,
                                         scale=vec[:, g:g + 1])
                ins.then_inc(s_wh, 1)

        def split_low(eng, ph, U, k):
            par, slot = k % 2, k % RING
            eng.wait_ge(s_wh, U + 1)
            n = ph.kts * ph.cw
            if ph.gcol is None:
                eng.tensor_tensor(WL[:, slot, 0:n], RAW[:, par, 0:n], WH[:, slot, 0:n].bitcast(F32),
                                  ALU.subtract).then_inc(s_wl, 1)
            else:
                for kt in range(ph.kts):
                    g = ph.gcol + (k % ph.upc) * ph.kts + kt
                    ins = eng.scalar_tensor_tensor(
                        out=wview(WL, slot, ph)[:, kt, :], in0=wview(RAW, par, ph)[:, kt, :],
                        scalar=vec[:, g:g + 1], in1=wview(WH, slot, ph)[:, kt, :].bitcast(F32),
                        op0=ALU.mult, op1=ALU.subtract)
                ins.then_inc(s_wl, 1)

        def ahead(split, eng, ph, U, k):
            if isinstance(U, int):
                if U + LEAD < UNITS:
                    nph, nk = TABLE[U + LEAD]
                    split(eng, nph, U + LEAD, nk)
            else:
                split(eng, ph, U + LEAD, (k + LEAD) % ph.upc)

        def three(pe, acc, wh, wl, xh, xl, first, last):
            pe.matmul(acc, wh, xh, start=first, stop=False)
            pe.matmul(acc, wh, xl, start=False, stop=False)
            return pe.matmul(acc, wl, xh, start=False, stop=last)

        s_memset = sem("constants_set")
        s_vecd, s_vect, s_vec = sem("vector_rows_loaded"), sem("vector_rows_turned"), sem("vectors_ready")
        s_act, s_dve, s_pool = sem("scalar_steps"), sem("vector_steps"), sem("gpsimd_steps")
        s_rowd = [sem(f"row_loaded{k}") for k in range(4)]
        s_memd = sem("memory_rows_loaded")
        s_resd = [sem(f"residual_loaded{k}") for k in range(3)]
        s_row = sem("row_normalised")
        s_xt, s_xh, s_xl = sem("rows_turned"), sem("turned_high"), sem("turned_low")
        s_sq, s_rs = sem("squares_summed"), sem("rstd_ready")
        s_bank = {n: sem(f"bank_full_{n}") for n in phases}
        s_ev = {n: sem(f"bank_emptied_{n}") for n in phases}
        s_st = {n: [sem(f"stage_stored_{n}{k}") for k in range(2)] for n in ("mem", "in_a", "in_b")}
        s_par, s_parT, s_parE = sem("params_loaded"), sem("params_turned"), sem("params_copied")
        s_zero = sem("zeros_set")
        s_trig, s_sin, s_pw = sem("angles_ready"), sem("sines_ready"), sem("powers_ready")

        ROW, JUNK, ROW_ = place([(2, D), (D,), (2, D)])
        OUTROW, GB, JUNK2, ss4, RES_ = place([(NT, D), (D,), (RW,), (2, NT, 4), (D,)], at=2 * D)
        ROWS_IN = [ROW[:, 0], ROW[:, 1], ROW_[:, 0], ROW_[:, 1]]
        RES = [ROW[:, 0], ROW[:, 1], RES_]
        (U, CR, SR, CTH, W, FS, FO, KDS, BVT, TZ, HPZ, PW, PB, BR, BV, TMP, CP, BB, DT, KA, DTS) = place(
            [(2 * JB, NC), (2, P), (2 * P,), (384,), (2, JB, NC), (2, NB + 1, JB), (2 * P,), (JB, P), (2 * JB * P,),
             (2 * JB, P), (2, 2, JB, NC), (NPW, 2, PAIRS), (NPW, 2, JB), (2, JB, GH), (2, JB, STEPS, GH),
             (JB * (STEPS + 1) * GH,), (2, JB, STEPS + 1, GH), (2, JB, 2, GH), (G,), (6, 2, JB), (2 * JB,)])

        def x_rows(t):
            if t < NT - 1:
                return io["x_prompt"][0, P * t:P * t + P, :].rearrange("(c s) d -> s c d", s=STEPS)
            return io["x_sample"].rearrange("b (k s) d -> s (b k) d", s=STEPS)

        def x_rows_plain(t):
            if t < NT - 1:
                return io["x_prompt"][0, P * t:P * t + P, :]
            return io["x_sample"].rearrange("b i d -> (b i) d")


        VROW = JUNK[:, 0:P]
        PRM = TMP[:, 0:384].rearrange("p (a m) -> p a m", a=3)
        PRL, DRW, PRD = TMP[:, 384:386], TMP[:, 400:416], TMP[:, 512:640]
        CPF = CP.rearrange("p a b c d -> p (a b c d)")
        WV = BVT
        KST = BVT[:, :].rearrange("p (x j c) -> p x j c", x=4, j=JB)
        YS = W[:, :, :, :].rearrange("p r j c -> p (r j) c")

        def CPT(k, n=1):
            return CPF[:, PAIRS * k:PAIRS * (k + n)]

        s_u, s_crd, s_brd = sem("u_loaded"), sem("c_rows_loaded"), sem("b_loaded")
        s_cT, s_cTe = sem("c_turned"), sem("c_copied")
        s_bv, s_cp, s_bb = sem("bv_ready"), sem("cp_ready"), sem("b_blocks_ready")
        s_wvT, s_wve = sem("wv_turned"), sem("wv_copied")
        s_V, s_Ve = sem("v_products"), sem("v_copied")
        s_kd, s_kde, s_kst, s_tz = sem("lags_product"), sem("lags_copied"), sem("lags_stored"), sem("tz_loaded")
        s_hp, s_fs, s_fT, s_fTe, s_fst = sem("states_ready"), sem("finals_ready"), sem("finals_turned"), sem("finals_copied"), sem("finals_stored")
        s_y, s_ye, s_yst = sem("y_products"), sem("y_ready"), sem("y_stored")

        def prime_ssm(pool):
            for k, (s, n) in enumerate(((s_ye, 3), (s_y, 3), (s_wvT, 1), (s_kd, 1), (s_cp, 1), (s_hp, 1), (s_cT, 1),
                         (s_fT, 1), (s_fTe, 1), (s_yst, 128), (s_fst, 32), (s_kst, 16), (s_kde, 1), (s_bb, 1))):
                pool.memset(marks[0:1, k + 1:k + 2], 0.0).then_inc(s, n)

        def ssm_params(dve, mine):
            dve.wait_ge(s_par, 64)
            mine(dve.tensor_copy(PRM[0:48, 2, :].rearrange("j (q p) -> j q p", q=2),
                                 PRL[0:48, :].unsqueeze(2).broadcast_to([48, 2, ST])))
            dve.tensor_copy(PRD[0:G, :].rearrange("g (t h) -> g t h", h=GH),
                            DRW[0:G, :].unsqueeze(1).broadcast_to([G, STEPS, GH])).then_inc(s_parE, 1)

        def ssm_params2(dve, mine):
            def step(ins):
                mine(ins)
                mine.wait()

            ts, tt, stt = dve.tensor_scalar, dve.tensor_tensor, dve.scalar_tensor_tensor

            def nearest(o, x, factor):
                step(ts(o, x, factor, 12582912.0, ALU.mult, ALU.add))
                step(ts(o, o, -12582912.0, None, ALU.add))

            def exp(o, x, k, r):
                step(ts(x, x, -87.0, 88.0, ALU.max, ALU.min))
                nearest(k, x, 1.4426950408889634)
                step(stt(out=r, in0=k, scalar=-0.693359375, in1=x, op0=ALU.mult, op1=ALU.add))
                step(stt(out=r, in0=k, scalar=2.12194440054690583e-4, in1=r, op0=ALU.mult, op1=ALU.add))
                step(ts(o, r, 1.0 / 5040, None, ALU.mult))
                for n in (720, 120, 24, 6, 2, 1):
                    step(stt(out=o, in0=o, scalar=1.0 / n, in1=r, op0=ALU.add, op1=ALU.mult))
                step(ts(k.bitcast(I32), k, 127.0, 8388608.0, ALU.add, ALU.mult))
                step(stt(out=o, in0=o, scalar=1.0, in1=k, op0=ALU.add, op1=ALU.mult))

            dve.wait_ge(s_parT, 1)
            mine(dve.tensor_copy(CPT(0, 3), PS[:, 7, 64:64 + 144]))
            step(dve.tensor_copy(DT, PS[:, 7, 208:208 + G]))
            lre, lim, ldt, dt, mag, ang, kk, r, rc, ra = (CPT(k) for k in (0, 1, 2, 3, 5, 6, 7, 8, 10, 9))
            exp(dt, ldt, kk, r)
            step(tt(CPT(4), lre, dt, ALU.mult))
            exp(mag, CPT(4), kk, r)
            step(tt(ang, lim, dt, ALU.mult))
            nearest(kk, ang, 1.0 / (2 * math.pi))
            step(stt(out=r, in0=kk, scalar=-6.28125, in1=ang, op0=ALU.mult, op1=ALU.add))
            step(stt(out=r, in0=kk, scalar=-0.0019350051879882812, in1=r, op0=ALU.mult, op1=ALU.add))
            step(stt(out=r, in0=kk, scalar=-3.0199157e-07, in1=r, op0=ALU.mult, op1=ALU.add))
            step(ts(r, r, -3.1415925, 3.1415925, ALU.max, ALU.min))
            step(stt(out=ra, in0=r, scalar=-1.0, in1=r, op0=ALU.mult, op1=ALU.max))
            dve.tensor_scalar(rc, ra, -1.0, math.pi / 2, ALU.mult, ALU.add).then_inc(s_trig, 1)

        def ssm_params3(dve, mine):
            def step(ins):
                mine(ins)
                mine.wait()

            ts, tt, stt = dve.tensor_scalar, dve.tensor_tensor, dve.scalar_tensor_tensor
            lre, lim, mag, sin, cos = (CPT(k) for k in (0, 1, 5, 11, 12))
            dve.wait_ge(s_sin, 1)
            step(tt(PW[:, 1, 0, :], mag, cos, ALU.mult))
            step(tt(PW[:, 1, 1, :], mag, sin, ALU.mult))
            step(dve.memset(PW[:, 0, 0, :], 1.0))
            step(dve.memset(PW[:, 0, 1, :], 0.0))
            nr, ni, den, t1, t2 = PW[:, 2, 0, :], PW[:, 1, 1, :], CPT(13), CPT(14), CPT(15)
            step(ts(nr, PW[:, 1, 0, :], -1.0, None, ALU.add))
            step(tt(t1, lre, lre, ALU.mult))
            step(tt(t2, lim, lim, ALU.mult))
            step(tt(den, t1, t2, ALU.add))
            step(dve.reciprocal(den, den))
            step(tt(t1, nr, lre, ALU.mult))
            step(tt(t2, ni, lim, ALU.mult))
            step(tt(t1, t1, t2, ALU.add))
            step(tt(CPT(16), t1, den, ALU.mult))
            step(tt(t1, ni, lre, ALU.mult))
            step(tt(t2, nr, lim, ALU.mult))
            step(tt(t1, t1, t2, ALU.subtract))
            dve.tensor_tensor(CPT(17), t1, den, ALU.mult).then_inc(s_pw, 1)

        def complex_product(eng, mine, dst, a, b, t, ready=None):
            tt = eng.tensor_tensor
            mine(tt(dst[0], a[0], b[0], ALU.mult))
            mine(tt(t, a[1], b[1], ALU.mult))
            mine.wait()
            mine(tt(dst[0], dst[0], t, ALU.subtract))
            mine.wait()
            mine(tt(dst[1], a[0], b[1], ALU.mult))
            mine(tt(t, a[1], b[0], ALU.mult))
            mine.wait()
            if ready is not None:
                tt(dst[1], dst[1], t, ALU.add).then_inc(ready, 1)
                return
            mine(tt(dst[1], dst[1], t, ALU.add))
            mine.wait()

        def ssm_params_pool(pool, mine):
            pool.wait_ge(s_pw, 1)

            def both(a, b):
                return PW[:, a:b, 0, :], PW[:, a:b, 1, :]

            def repeated(v, n):
                return tuple(x.broadcast_to([P, n, PAIRS]) for x in v)

            t = TMP[:, 0:384].rearrange("p (k j) -> p k j", k=8)
            complex_product(pool, mine, both(2, 3), both(1, 2), both(1, 2), t[:, 0:1, :])
            complex_product(pool, mine, both(3, 5), both(1, 3), repeated(both(2, 3), 2), t[:, 0:2, :])
            complex_product(pool, mine, both(5, 9), both(1, 5), repeated(both(4, 5), 4), t[:, 0:4, :])
            q = tuple(CPT(k).unsqueeze(1).broadcast_to([P, 8, PAIRS]) for k in (16, 17))
            back = tuple(PW[:, 7::-1, k, :] for k in range(2))
            complex_product(pool, mine, both(9, 17), back, q, t)
            mine(pool.tensor_copy(PW[:, 17, :, :], PW[:, 8, :, :]))
            mine.wait()
            for k in range(17, 22):
                complex_product(pool, mine, both(k + 1, k + 2), both(k, k + 1), both(k, k + 1), t[:, 0:1, :])

        def ssm_pool(pool, mine, i):
            pool.wait_ge(s_cT, i + 1)
            pool.wait_ge(s_memset, 1)
            for q in range(2):
                for j, name in enumerate(("ssm_c_re", "ssm_c_im")):
                    src = io[name][0].rearrange("(x j q) h p -> x q j h p", q=2, j=JB)[ds(i, 1), q].rearrange("o j h p -> (o j) h p")
                    pool.dma_start(CR[:, j, q * ST:q * ST + ST], src).then_inc(s_crd, 16)
            src = io["state_ssm"][0].rearrange("b (x j q) p r -> x b j (q p r)", q=2, j=JB)[ds(i, 1)].rearrange("o b j f -> (o b) j f")
            pool.dma_start(SR[0:64, :], src).then_inc(s_crd, 16)
            for j, name in enumerate(("ssm_b_re", "ssm_b_im")):
                src = io[name][0].rearrange("(x j q) p h -> x (q p) j h", q=2, j=JB)[ds(i, 1)].rearrange("o m j h -> (o m) j h")
                pool.dma_start(BR[:, j, :, :], src).then_inc(s_brd, 16)
            mine(pool.tensor_copy(PB[:], PW[:, :, :, ds(i * JB, JB)]))
            mine.wait()
            pool.wait_ge(s_brd, i * 32 + 32)
            pool.wait_ge(s_wvT, i + 1)
            pool.wait_ge(s_bb, i + 1)
            full = [P, JB, STEPS, GH]
            b = tuple(BR[:, k, :, :].unsqueeze(2).broadcast_to(full) for k in range(2))
            qa = tuple(PB[:, 9:17, k, :].rearrange("p s j -> p j s").unsqueeze(3).broadcast_to(full) for k in range(2))
            t = TMP[:, 0:JB * STEPS * GH].rearrange("p (j s h) -> p j s h", j=JB, s=STEPS)
            complex_product(pool, mine, (BV[:, 0], BV[:, 1]), b, qa, t, s_bv)
            pool.wait_ge(s_bv, i + 1)
            pool.wait_ge(s_cTe, i + 1)
            pool.wait_ge(s_y, i * 3 + 3)
            full = [P, JB, STEPS + 1, GH]
            c = tuple(CTH[:, k * P:(k + 1) * P].rearrange("p (j h) -> p j h", h=GH).unsqueeze(2).broadcast_to(full) for k in range(2))
            a = tuple(PB[:, 0:9, k, :].rearrange("p s j -> p j s").unsqueeze(3).broadcast_to(full) for k in range(2))
            t = TMP[:].rearrange("p (j s h) -> p j s h", j=JB, s=STEPS + 1)
            tt = pool.tensor_tensor
            mine(tt(CP[:, 0], c[0], a[0], ALU.mult))
            mine(tt(t, c[1], a[1], ALU.mult))
            mine.wait()
            mine(tt(CP[:, 0], CP[:, 0], t, ALU.add))
            mine.wait()
            mine(tt(CP[:, 1], c[1], a[0], ALU.mult))
            mine(tt(t, c[0], a[1], ALU.mult))
            mine.wait()
            pool.tensor_tensor(CP[:, 1], CP[:, 1], t, ALU.subtract).then_inc(s_cp, 1)

        def ssm_pe(pe, ph, i):
            def turn_c():
                pe.wait_ge(s_crd, i * 80 + 80)
                pe.wait_ge(s_ye, i * 3 + 3)
                for k in range(2):
                    pe.transpose(PS[:, 4, k * P:k * P + P], CR[:, k, :], ident[:])
                for k in range(2):
                    ins = pe.transpose(PS[:, 4, 256 + 64 * k:320 + 64 * k],
                                       SR[0:64, :].rearrange("b (m r) -> b r m", r=2)[:, k, :], ident[0:64, 0:64])
                ins.then_inc(s_cT, 1)

            def turn_bv():
                pe.wait_ge(s_bv, i + 1)
                pe.wait_ge(s_cTe, i + 1)
                pe.wait_ge(s_fTe, i + 1)
                for x in range(4):
                    for j in range(4):
                        r, jj = x // 2, 4 * (x % 2) + j
                        ins = pe.transpose(PS[:, 4 + x, j * P:j * P + P], BV[:, r, jj].rearrange("p s h -> p (s h)"), ident[:])
                ins.then_inc(s_wvT, 1)

            def products_v(part):
                if part == 0:
                    pe.wait_ge(s_u, i * 128 + 128)
                    pe.wait_ge(s_wve, i * 4 + 4)
                else:
                    pe.wait_ge(s_Ve, i * 2 + 1)
                for j in range(4):
                    jj = 4 * part + j
                    for r in range(2):
                        c = r * 2 * NC
                        ins = pe.matmul(PS[:, 4 + j, c:c + 2 * NC], WV[:, (r * JB + jj) * P:(r * JB + jj + 1) * P],
                                        U[:, 2 * jj:2 * jj + 2, :].rearrange("p q c -> p (q c)"), start=(r == 0), stop=True,
                                        skip_group_check=True)
                ins.then_inc(s_V, 1)

            def products_lags():
                pe.wait_ge(s_cp, i + 2)
                pe.wait_ge(s_bb, i + 2)
                pe.wait_ge(s_Ve, i * 2 + 2)
                for j in range(JB):
                    o = PS[0:32, 4 + j // 4, (j % 4) * P:(j % 4 + 1) * P]
                    for r in range(2):
                        ins = pe.matmul(o, BB[:, r, j].rearrange("p q h -> p (q h)"),
                                        CP[:, r, j, 0:8].rearrange("p k h -> p (k h)"),
                                        start=(r == 0 and j % 4 == 0), stop=(r == 1), skip_group_check=True)
                ins.then_inc(s_kd, 1)

            def products_y():
                pe.wait_ge(s_tz, i * 128 + 128)
                pe.wait_ge(s_kde, i + 2)
                for g in range(2 * JB):
                    o = PS[:, 4 + g // 6, (g % 6) * NC:(g % 6 + 1) * NC]
                    pe.matmul(o, TZ[:, g, :], U[:, g, :], start=(g % 6 == 0), stop=False, skip_group_check=True)
                pe.wait_ge(s_hp, i + 2)
                for j in range(JB):
                    o = PS[:, 4 + j // 3, (j % 3) * 2 * NC:(j % 3 + 1) * 2 * NC].rearrange("p (q c) -> p q c", q=2)
                    for r in range(2):
                        ins = pe.matmul(o, CP[:, r, j, 1:9].rearrange("p k h -> p (k h)"), HPZ[:, r, :, j, :],
                                        start=False, stop=(r == 1), skip_group_check=True)
                    if j in (2, 5, 7):
                        ins.then_inc(s_y, 1)
                pe.wait_ge(s_fs, i + 1)
                for r in range(2):
                    ins = pe.transpose(PS[0:72, 7, r * P:r * P + P], FS[:, r].rearrange("p b j -> p (b j)"), ident[:])
                ins.then_inc(s_fT, 1)

            aux = {0: [turn_c], 1: [turn_bv], 3: [lambda: products_v(0)], 4: [products_lags]}
            for x in range(8):
                for f in aux.get(x, ()):
                    f()
                n = i * 2 + 1 + x // 4
                unit_stationary(pe, ph, (i * 2 + 1 + x // 4) * 4 + ph.first + x % 4, x % 4, n,
                                (lambda q: products_v(1) if q == 2 else None) if x == 3 else None)
            products_y()

        def ssm_act(act, mine, i):
            def early():
                act.wait_ge(s_cT, i + 2)
                act.wait_ge(s_cp, i + 1)
                act.wait_ge(s_hp, i + 1)
                act.activation(CTH[:, 0:P], PS[:, 4, 0:P], ACT.Copy)
                act.activation(CTH[:, P:2 * P], PS[:, 4, P:2 * P], ACT.Copy, scale=-1.0)
                act.activation(CTH[:, 2 * P:384], PS[:, 4, 2 * P:384], ACT.Copy).then_inc(s_cTe, 1)

            def second():
                act.wait_ge(s_zero, 3)
                act.wait_ge(s_bv, i + 1)
                act.wait_ge(s_kd, i + 1)
                for q in range(2):
                    r = slice(q * ST, q * ST + ST)
                    ins = act.activation(BB[r, :, :, q, :], BV[r, :, :, STEPS - 1, :], ACT.Copy)
                ins.then_inc(s_bb, 1)
                for m in range(2):
                    act.wait_ge(s_st["in_a"][m], i * 32 + 16)
                act.wait_ge(s_ye, i * 3 + 3)
                src = scr["in_a"][ds(i * 2, 2)].rearrange("m (g h) (s c) -> s h (m g) c", h=GH, s=STEPS)
                for s in range(STEPS):
                    act.dma_start(U[s * GH:s * GH + GH, :, :], src[s]).then_inc(s_u, 16)
                act.wait_ge(s_wvT, i + 2)
                for x in range(4):
                    act.activation(WV[:, x * 512:(x + 1) * 512], PS[:, 4 + x, :], ACT.Copy).then_inc(s_wve, 1)

            def copy_v():
                for part in range(2):
                    act.wait_ge(s_V, i * 2 + 1 + part)
                    if part == 0:
                        act.wait_ge(s_yst, i * 128 + 128)
                    for j in range(4):
                        for q in range(2):
                            r = slice(q * ST, q * ST + ST)
                            ins = act.activation(W[r, :, 4 * part + j, :],
                                                 PS[r, 4 + j, 0:320].rearrange("p (r q c) -> p r q c", r=2, q=2)[:, :, q, :], ACT.Copy)
                    ins.then_inc(s_Ve, 1)

            def lags():
                act.wait_ge(s_kd, i + 2)
                act.wait_ge(s_kst, i * 16 + 16)
                for x in range(2):
                    ins = act.activation(KDS[0:32, 4 * x:4 * x + 4, :],
                                         PS[0:32, 4 + x, :].rearrange("p (j m) -> p j m", j=4), ACT.Copy)
                ins.then_inc(s_kde, 1)
                act.wait_ge(s_kde, i + 2)
                dst = scr["lags"].rearrange("(x j q) h m -> x (q h) j m", j=JB, q=2)[ds(i, 1)].rearrange("o a j m -> (o a) j m")
                act.dma_start(dst, KDS[0:32]).then_inc(s_kst, 16)

            def spread_lags():
                act.wait_ge(s_zero, 3)
                act.wait_ge(s_kst, i * 16 + 32)
                act.wait_ge(s_y, i * 3 + 3)
                src = scr["lags"].rearrange("(x g) h m -> x h g m", g=2 * JB)[ds(i, 1)].rearrange("o h g m -> (o h) g m")
                for s in range(STEPS):
                    act.dma_start(TZ[s * GH:s * GH + GH, :, s * GH:P], src[:, :, 0:P - s * GH]).then_inc(s_tz, 16)

            def late():
                act.wait_ge(s_fT, i + 2)
                act.wait_ge(s_fst, i * 32 + 32)
                act.activation(FO[0:72, :].rearrange("b (m r) -> b r m", r=2),
                               PS[0:72, 7, 0:2 * P].rearrange("b (r m) -> b r m", r=2), ACT.Copy).then_inc(s_fTe, 1)
                act.wait_ge(s_fTe, i + 2)
                dst = out["ssm_sample"][0].rearrange("b (x j q) p r -> x b j (q p r)", q=2, j=JB)[ds(i, 1)].rearrange("o b j f -> (o b) j f")
                act.dma_start(dst, FO[0:64, :]).then_inc(s_fst, 16)
                dst = out["ssm_prompt"][0, 0].rearrange("(x j q) p r -> x j (q p r)", q=2, j=JB)[ds(i, 1)].rearrange("o j f -> (o j) f")
                act.dma_start(dst, FO[64:72, :]).then_inc(s_fst, 16)
                act.wait_ge(s_ye, i * 3 + 6)
                dst = scr["y"].rearrange("(x g) h (t c) -> x t h g c", g=2 * JB, t=STEPS)[ds(i, 1)].rearrange("o t h g c -> (o t) h g c")
                for t in range(STEPS):
                    act.dma_start(dst[t], YS[t * GH:t * GH + GH, :, :]).then_inc(s_yst, 16)

            return [early, second, None, copy_v, lags, spread_lags, None, None, late]

        def ssm_dve(dve, mine, i):
            tt = dve.tensor_tensor

            def level(lv):
                s = 1 << lv
                n = PC - s
                a = tuple(KA[:, lv, k, :].unsqueeze(2).broadcast_to([P, JB, n]) for k in range(2))
                old = tuple(W[:, k, :, 0:n] for k in range(2))
                t = [KST[:, k, :, 0:n] for k in range(4)]
                mine(tt(t[0], old[0], a[0], ALU.mult))
                mine(tt(t[1], old[1], a[1], ALU.mult))
                mine(tt(t[2], old[0], a[1], ALU.mult))
                mine(tt(t[3], old[1], a[0], ALU.mult))
                mine.wait()
                mine(tt(t[0], t[0], t[1], ALU.subtract))
                mine(tt(t[2], t[2], t[3], ALU.add))
                mine.wait()
                for k in range(2):
                    new = W[:, k, :, s:PC]
                    mine(tt(new, new, t[2 * k], ALU.add))
                mine.wait()

            def tables():
                mine(dve.tensor_copy(KA[:], PW[:, 17:23, :, ds(i * JB, JB)]))
                mine(dve.tensor_copy(DTS[:], DT[:, ds(i * 2 * JB, 2 * JB)]))
                mine.wait()

            def first():
                dve.wait_ge(s_Ve, i * 2 + 2)
                level(0)
                level(1)

            def second():
                level(2)
                level(3)

            def third():
                level(4)
                level(5)

            def fourth():
                a = tuple(KA[:, 0, k, :].unsqueeze(2).broadcast_to([P, JB, NB]) for k in range(2))
                sample = W[:, :, :, PC:NC].rearrange("p r j (b k) -> p r j b k", k=2)
                h0 = CTH[:, 2 * P:384].rearrange("p (r b j) -> p r j b", r=2, b=NB)
                t = [KST[:, k, :, 0:NB] for k in range(4)]
                for step in range(2):
                    h = [h0[:, r] if step == 0 else sample[:, r, :, :, 0] for r in range(2)]
                    mine(tt(t[0], h[0], a[0], ALU.mult))
                    mine(tt(t[1], h[1], a[1], ALU.mult))
                    mine(tt(t[2], h[0], a[1], ALU.mult))
                    mine(tt(t[3], h[1], a[0], ALU.mult))
                    mine.wait()
                    mine(tt(t[0], t[0], t[1], ALU.subtract))
                    mine(tt(t[2], t[2], t[3], ALU.add))
                    mine.wait()
                    for k in range(2):
                        new = sample[:, k, :, :, step]
                        mine(tt(new, new, t[2 * k], ALU.add))
                    mine.wait()
                dve.wait_ge(s_y, i * 3 + 3)
                dve.wait_ge(s_zero, 3)
                for q in range(2):
                    r = slice(q * ST, q * ST + ST)
                    dve.tensor_copy(HPZ[r, :, q, :, 1:PC], W[r, :, :, 0:PC - 1])
                    new = HPZ[r, :, q, :, PC:NC].rearrange("p r j (b k) -> p r j b k", k=2)
                    dve.tensor_copy(new[:, :, :, :, 0], h0[r])
                    for k in range(2):
                        ins = dve.tensor_copy(new[:, k, :, :, 1], sample[r, k, :, :, 0])
                ins.then_inc(s_hp, 1)
                dve.wait_ge(s_fT, i + 1)
                for k in range(2):
                    dve.tensor_copy(FS[:, k, 0:NB, :], sample[:, k, :, :, 1].rearrange("p j b -> p b j"))
                mine(dve.tensor_copy(FS[:, :, NB, :], W[:, :, :, PC - 1]))
                mine.wait()
                dve.wait_ge(s_u, i * 128 + 128)
                dve.tensor_tensor(YS, U[:], DTS[:].unsqueeze(2).broadcast_to([P, 2 * JB, NC]), ALU.mult).then_inc(s_fs, 1)
                dve.wait_ge(s_fs, i + 1)

            def late():
                for x, n in ((0, 6), (1, 6), (2, 4)):
                    dve.wait_ge(s_y, i * 3 + 4 + x)
                    o = YS[:, 6 * x:6 * x + n, :]
                    tt(o, o, PS[:, 4 + x, 0:n * NC].rearrange("p (g c) -> p g c", c=NC), ALU.add).then_inc(s_ye, 1)

            return [tables, None, None, first, second, third, fourth, None, late]

        MS, MROWS, MPR, MPT, sm = place([(MH, TOK), (5, 2, MEMW), (MH, NM), (2, MH, P), (2, 4, MH)])
        QRAW, = place([(MH, TOK)], at=MH * TOK + 3 * 2 * MEMW)
        GTMP = [FA[:, FN - KT * TOK - TOK:FN - KT * TOK], MPT[:].rearrange("p t h m -> p (t h m)")[:, 0:TOK]]
        MQ, AM = place([(MH, TOK), (MIXB, TOK)], at=FN - KT * TOK)

        def KTM(t):
            return MROWS[:, 3 + t % 2].rearrange("p t (h m) -> p (t h m)", h=MH).rearrange("p (h m) -> p h m", h=MH)

        MEM_STEPS = [(4, "K", 0), (6, "S", 0), (8, "S", 1), (9, "P", 0), (10, "A", 0), (12, "S", 2), (13, "P", 1), (14, "A", 1),
                   (16, "S", 3), (17, "P", 2), (18, "A", 2), (19, "K", 1), (20, "K", 2), (21, "P", 3), (22, "s", 0),
                   (22, "A", 3), (23, "s", 1), (23, "K", 3), (24, "s", 2), (24, "K", 4), (25, "s", 3), (25, "K", 5),
                   (26, "s", 4), (26, "K", 6), (27, "s", 5), (27, "K", 7), (28, "s", 6), (28, "K", 8), (29, "s", 7),
                   (30, "T", 4), (33, "P", 4), (34, "V", 0), (34, "V", 1), (34, "V", 2), (35, "V", 3), (35, "V", 4),
                   (35, "V", 5), (35, "V", 6), (35, "V", 7)]
        TURNS = [(k, t) for _, k, t in MEM_STEPS if k in "KP" or (k, t) == ("s", NB - 1)]
        TURN = {x: n for n, x in enumerate(TURNS)}
        ROWS = [("K", 0, 0), ("V", -1, 1)] + [("K", b, (b + 1) % 3) for b in range(1, NB + 1)] + \
            [("V", b, (1, 2, 0, 4, 3, 1, 2, 0)[b]) for b in range(NB)]
        NTH = {(k, b): sum(1 for y in ROWS[:n] if y[2] == sl) + 1 for n, (k, b, sl) in enumerate(ROWS)}
        SLOT = {(k, b): sl for k, b, sl in ROWS}
        PER_LAYER = {"q_loaded": 16, "q_ordered": 1, "g_loaded": 16, "gate_sigmoid": 4, "gate_ready": 4,
                     "turned": len(TURNS), "high_copied": len(TURNS), "low_copied": len(TURNS), "scores": 5, "negmax": 5, "exps": 5, "probs": 5,
                     "values": 4, "value_stream": 8, "gated": 5}
        PER_LAYER |= {f"rows{k}": 16 * sum(1 for y in ROWS if y[2] == k) for k in range(5)}
        mm = {n: sem(f"mem_{n}") for n in PER_LAYER}

        def layer_wait(eng, l, name, count):
            eng.wait_ge(mm[name], l * PER_LAYER[name] + count)

        SRC = ("in_a", "in_b")
        DST = ("out_a", "out_b")

        def natural(v):
            return v.rearrange("p (c s) -> p s c", s=STEPS)

        def by_step(v):
            return v.rearrange("p (s c) -> p s c", s=STEPS)

        def stream_cols(v, b):
            return v[:, DSEQ * b:DSEQ * b + DSEQ]

        def mem_copied(eng, l, x):
            layer_wait(eng, l, "high_copied", TURN[x] + 1)
            layer_wait(eng, l, "low_copied", TURN[x] + 1)

        def mem_pe(pe, l, place_):
            for kind, t in [(k, t) for q, k, t in MEM_STEPS if q == place_]:
                if kind in "KP":
                    n = TURN[kind, t]
                    if n and TURNS[n - 1][0] != "s":
                        mem_copied(pe, l, TURNS[n - 1])
                    if n and TURNS[n - 1][0] == "P":
                        layer_wait(pe, l, "gated", TURNS[n - 1][1] + 1)
                    if kind == "K":
                        layer_wait(pe, l, f"rows{SLOT['K', t]}", 16 * NTH["K", t])
                        src = MROWS[:, SLOT["K", t]]
                        tiles = [[src[:, mt, h * P:h * P + P] for h in range(MH)] for mt in range(2)]
                    else:
                        layer_wait(pe, l, "probs", t + 1)
                        tiles = [[MPR[:, h, mt * P:mt * P + P] for h in range(MH)] for mt in range(2)]
                    for mt in range(2):
                        for h in range(MH):
                            ins = pe.transpose(PS[:, 6 + mt, h * P:h * P + P], tiles[mt][h], ident[:])
                    ins.then_inc(mm["turned"], 1)
                elif kind == "S":
                    mem_copied(pe, l, ("K", 0))
                    if t == 0:
                        layer_wait(pe, l, "q_loaded", 16)
                        layer_wait(pe, 0, "q_ordered", 1)
                    else:
                        layer_wait(pe, l, "exps", t)
                    for h in range(MH):
                        ins = pe.matmul(PS[:, 4 + h // 2, (h % 2) * NM:(h % 2 + 1) * NM], MQ[:, h, P * t:P * t + P],
                                        KTM(0)[:, h, :], start=(h % 2 == 0), stop=True, skip_group_check=True)
                    ins.then_inc(mm["scores"], 1)
                elif kind == "s":
                    mem_copied(pe, l, ("K", t + 1))
                    if t == 0:
                        layer_wait(pe, l, "exps", 4)
                    for mt in range(2):
                        for h in range(MH):
                            ins = pe.matmul(stream_cols(PS[:, 4 + mt, h * P:h * P + P], t), KTM(t + 1)[:, h, mt * P:mt * P + P],
                                            stream_cols(MQ[:, h, SEQ:TOK], t), start=(t == 0 and h == 0), stop=True,
                                            skip_group_check=True)
                    if t == NB - 1:
                        ins.then_inc(mm["turned"], 1)
                elif kind == "T":
                    mem_copied(pe, l, ("s", NB - 1))
                    for mt in range(2):
                        for h in range(MH):
                            ins = pe.transpose(PS[:, 4 + h // 2, (h % 2) * NM + mt * P:(h % 2) * NM + mt * P + P], MPT[:, mt, h, :], ident[:])
                    ins.then_inc(mm["scores"], 1)
                elif kind == "A":
                    mem_copied(pe, l, ("P", t))
                    layer_wait(pe, l, "rows1", 16)
                    for h in range(MH):
                        for mt in range(2):
                            ins = pe.matmul(PS[:, 6, h * P:h * P + P], MROWS[:, 1, mt, h * P:h * P + P], MPT[:, mt, h, :],
                                            start=(h == 0 and mt == 0), stop=(mt == 1), skip_group_check=True)
                    ins.then_inc(mm["values"], 1)
                else:
                    mem_copied(pe, l, ("P", NT - 1))
                    layer_wait(pe, l, f"rows{SLOT['V', t]}", 16 * NTH["V", t])
                    for h in range(MH):
                        for mt in range(2):
                            ins = pe.matmul(stream_cols(PS[:, 6, h * P:h * P + P], t), MROWS[:, SLOT["V", t], mt, h * P:h * P + P],
                                            stream_cols(MPT[:, mt, h, :], t),
                                            start=(t == 0 and h == 0 and mt == 0), stop=(mt == 1), skip_group_check=True)
                    ins.then_inc(mm["value_stream"], 1)

        def mem_gates_act(act, l):
            layer_wait(act, l, "g_loaded", 16)
            for h in range(MH):
                if h >= 2:
                    layer_wait(act, l, "gate_ready", h - 1)
                act.activation(GTMP[h % 2], MS[:, h, :], ACT.Sigmoid).then_inc(mm["gate_sigmoid"], 1)

        def mem_gates_dve(dve, l):
            for h in range(MH):
                layer_wait(dve, l, "gate_sigmoid", h + 1)
                dve.tensor_tensor(MS[:, h, :], MS[:, h, :], GTMP[h % 2], ALU.mult).then_inc(mm["gate_ready"], 1)

        def mem_queries_dve(dve, l):
            if l == 0:
                layer_wait(dve, l, "q_loaded", 16)
                for h in range(MH):
                    ins = dve.tensor_copy(natural(MQ[:, h, :]), by_step(QRAW[:, h, :]))
                ins.then_inc(mm["q_ordered"], 1)

        def tile_of_banks(a):
            return PS[:, a, :].rearrange("p (h m) -> p h m", h=MH)

        def mem_act(act, l, unit):
            def exps(t):
                layer_wait(act, l, "negmax", t + 1)
                if t:
                    layer_wait(act, l, "turned", TURN["P", t - 1] + 1)
                else:
                    layer_wait(act, 0, "q_ordered", 1)
                for h in range(MH):
                    ins = act.activation(MPR[:, h, :], PS[:, 4 + h // 2, (h % 2) * NM:(h % 2 + 1) * NM], ACT.Exp,
                                         bias=sm[:, t % 2, 1, h:h + 1], scale=SCALE, accum_out=sm[:, t % 2, 2, h:h + 1])
                ins.then_inc(mm["exps"], 1)

            for kind, t in [(k, t) for q, k, t in MEM_STEPS if q // 4 == unit]:
                if (kind, t) in TURN:
                    layer_wait(act, l, "turned", TURN[kind, t] + 1)
                if kind == "K":
                    if t == 0:
                        layer_wait(act, 0, "q_ordered", 1)
                    act.activation(KTM(t)[:, :, 0:P], tile_of_banks(6), ACT.Copy).then_inc(mm["high_copied"], 1)
                elif kind == "P":
                    if t:
                        layer_wait(act, l, "values", min(t, NT - 1))
                    else:
                        layer_wait(act, l, "gate_ready", MH)
                    act.activation(MPT[:, 0, :, :], tile_of_banks(6), ACT.Copy).then_inc(mm["high_copied"], 1)
                    if t < NT - 2:
                        exps(t + 1)
                elif kind == "s" and t == NB - 1:
                    layer_wait(act, l, "values", NT - 1)
                    act.activation(MPT[:, 0, :, :], tile_of_banks(4), ACT.Copy).then_inc(mm["high_copied"], 1)
                elif kind == "T" or (kind, t) == ("S", 0):
                    exps(t)

        def mem_dve(dve, mine, l, unit):
            def maxima(t):
                layer_wait(dve, l, "scores", t + 1)
                mine(dve.tensor_reduce(sm[:, t % 2, 0, :], PS[:, 4:6, :].rearrange("p b (h m) -> p (b h) m", h=2), AX.X, ALU.max))
                mine.wait()
                dve.tensor_scalar(sm[:, t % 2, 1, :], sm[:, t % 2, 0, :], -SCALE, None, ALU.mult).then_inc(mm["negmax"], 1)

            def probs(t):
                layer_wait(dve, l, "exps", t + 1)
                mine(dve.reciprocal(sm[:, t % 2, 3, :], sm[:, t % 2, 2, :]))
                mine.wait()
                dve.tensor_tensor(MPR[:], MPR[:], sm[:, t % 2, 3, :].unsqueeze(2).broadcast_to([P, MH, NM]), ALU.mult).then_inc(mm["probs"], 1)

            def gated(t):
                if t == 0:
                    layer_wait(dve, l, "gate_ready", MH)
                for h in range(0, MH, 2 if l == 0 else MH):
                    dst, o = MQ[:, :, P * t:P * t + P], tile_of_banks(6)
                    if l == 0:
                        hh = slice(h, h + 2)
                        dst, o = (v[:, hh].rearrange("p h (c s) -> p h c s", s=STEPS) for v in (dst, o))
                        g = MS[:, hh].rearrange("p h (s c) -> p h c s", s=STEPS)[:, :, 16 * t:16 * t + 16, :]
                    else:
                        g = MS[:, :, P * t:P * t + P]
                    ins = dve.tensor_tensor(dst, o, g, ALU.mult)
                ins.then_inc(mm["gated"], 1)

            for kind, t in [(k, t) for q, k, t in MEM_STEPS if q // 4 == unit]:
                if (kind, t) in TURN:
                    layer_wait(dve, l, "turned", TURN[kind, t] + 1)
                if kind == "K":
                    if t == 0:
                        layer_wait(dve, 0, "q_ordered", 1)
                    dve.tensor_copy(KTM(t)[:, :, P:2 * P], tile_of_banks(7)).then_inc(mm["low_copied"], 1)
                elif kind == "P":
                    if t:
                        layer_wait(dve, l, "values", min(t, NT - 1))
                    else:
                        layer_wait(dve, l, "gate_ready", MH)
                    dve.tensor_copy(MPT[:, 1, :, :], tile_of_banks(7)).then_inc(mm["low_copied"], 1)
                    if t < NT - 2:
                        maxima(t + 1)
                elif kind == "s" and t == NB - 1:
                    layer_wait(dve, l, "values", NT - 1)
                    dve.tensor_copy(MPT[:, 1, :, :], tile_of_banks(5)).then_inc(mm["low_copied"], 1)
                elif kind == "T" or (kind, t) == ("S", 0):
                    maxima(t)
                    probs(t)
                elif kind == "A":
                    layer_wait(dve, l, "values", t + 1)
                    gated(t)
                    if t < NT - 2:
                        probs(t + 1)
                elif (kind, t) == ("V", NB - 1):
                    layer_wait(dve, l, "value_stream", NB)
                    gated(NT - 1)

        def mem_pool(pool, l, then):
            for n, (kind, b, slot) in enumerate(ROWS):
                if n == 1:
                    pool.dma_start(QRAW if l == 0 else MQ[:], scr[SRC[l]][2 * MIXB:2 * MIXB + MH].rearrange("k p n -> p k n")).then_inc(mm["q_loaded"], 16)
                    pool.dma_start(MS[:], scr[SRC[l]][2 * MIXB + MH:NBLK].rearrange("k p n -> p k n")).then_inc(mm["g_loaded"], 16)
                if n == 4:
                    then()
                last = [y for y in ROWS[:n] if y[2] == slot][-1:]
                if slot >= 3:
                    last = [("s", NB - 1, 0)]
                for k, x, _ in last:
                    if (k, x) in TURN:
                        layer_wait(pool, l, "turned", TURN[k, x] + 1)
                    elif x < 0:
                        layer_wait(pool, l, "values", NT - 1)
                    else:
                        layer_wait(pool, l, "value_stream", x + 1)
                if kind == "K":
                    src = out["mem_k_prompt"][l, 0] if b == 0 else io["cache_mem_k"][l, b - 1]
                else:
                    src = out["mem_v_prompt"][l, 0] if b < 0 else io["cache_mem_v"][l, b]
                pool.dma_start(MROWS[:, slot], src.rearrange("(t p) h d -> p t (h d)", p=P)).then_inc(mm[f"rows{slot}"], 16)

        s_fh, s_fl, s_gel = sem("fill_high"), sem("fill_low"), sem("gelu_done")
        s_gt, s_gs, s_gm = [sem(f"gate_loaded{k}") for k in range(2)], sem("gate_sigmoid"), sem("gate_multiplied")
        s_gd, s_gd1, s_gd2, s_gsq, s_gq = (sem(f"b_gate_{n}") for n in ("once", "sigmoid", "twice", "quarter", "quarter_used"))
        s_am, s_gb_ld = [sem(f"branch_loaded{k}") for k in range(3)], sem("gate_block_loaded")
        SG, GT, GS = place([(2, TOK), (2, TOK), (2, TOK)])
        GB1, = place([(TOK,)], at=FN - KT * TOK - TOK)
        F_Y, F_A, F_B = 0, MIXB, MIXB + KT
        ORDER_A = list(range(MIXB, KT)) + list(range(MIXB))
        GATE_BLOCKS = [0, 1, 8, 9, 10, 11]
        ORDER_B = [0, 1, 2, 3, 4, 5, 8, 9, 10, 11, 6, 7, 12, 13, 14, 15]

        def branch(k):
            return AM[:, k, :] if k < MIXB else MQ[:, k - MIXB, :]

        def fill_views(first, k):
            xh, xl, e = XH[:, k, :], XL[:, k, :], branch(k)
            if first == F_A and k < MIXB:
                xh, xl, e = natural(xh), natural(xl), by_step(e)
            return xh, xl, e

        def fill_high(act, first, k):
            xh, xl, e = fill_views(first, k)
            act.activation(xh, e, ACT.Copy).then_inc(s_fh, 1)

        def fill_low(dve, first, n, k):
            xh, xl, e = fill_views(first, k)
            dve.wait_ge(s_fh, first + n + 1)
            dve.tensor_tensor(xl, e, xh.bitcast(F32), ALU.subtract).then_inc(s_fl, 1)

        s_osq = [sem(f"out_squared{l}") for l in range(2)]
        s_osum, s_x1, s_x1st = sem("out_summed"), sem("residual_ready"), sem("x1_stored")
        s_gb = sem("g_post_loaded")
        KV_STAGE, = place([(NT, RW)])
        s_kvst = [sem(f"kv_stored{t}") for t in range(NT)]

        KR, VR, KTB, QR, QT, TP, SP_, WT, SUM1, SUM0, OS = place(
            [(13, P), (13, P), (13, P), (TOK,), (TOK,), (3, 512), (3, 512), (3, 512), (2 * P,), (3 * P,), (TOK,)])
        s_q, s_qt, s_kr, s_vr = sem("q_rows"), sem("q_scaled"), sem("k_rows"), sem("v_rows")
        s_kt, s_kte, s_z, s_t = sem("k_turned"), sem("k_copied"), sem("z_ready"), sem("softplus_tail")
        s_sp, s_spm, s_sum, s_e = sem("softplus_ready"), sem("softplus_masked"), sem("later_sums"), sem("exponent_ready")
        s_w, s_wm, s_o, s_oe, s_ost = sem("weights_exp"), sem("weights_masked"), sem("head_product"), sem("head_copied"), sem("head_stored")

        DIAG = [(0, 0), (1, 0), (2, 0), (2, 2 * P)]
        NEW = (1, 3 * P)

        def sb_pe(pe, i, r):
            h = i * 2 + r

            def turn():
                pe.wait_ge(s_kr, h * 48 + 48)
                pe.wait_ge(s_oe, h * 2 + 2)
                for x in range(4):
                    for j in range(4 * x, min(4 * x + 4, 13)):
                        ins = pe.transpose(PS[:, 4 + x, (j % 4) * P:(j % 4 + 1) * P], KR[:, j, :], ident[:])
                    ins.then_inc(s_kt, 1)

            def scores():
                pe.wait_ge(s_kte, h * 4 + 4)
                pe.wait_ge(s_qt, h + 2)
                pe.matmul(PS[:, 4, :], KTB[:, 0, :], QT[:, 0:SEQ], start=True, stop=False, skip_group_check=True)
                pe.matmul(PS[:, 5, 0:3 * P], KTB[:, 1, :], QT[:, P:SEQ], start=True, stop=False, skip_group_check=True)
                pe.matmul(PS[:, 5, 3 * P:], KTB[:, 4, :], QT[:, SEQ:TOK], start=False, stop=False, skip_group_check=True)
                pe.matmul(PS[:, 6, 0:2 * P], KTB[:, 2, :], QT[:, 2 * P:SEQ], start=True, stop=False, skip_group_check=True)
                pe.matmul(PS[:, 6, 2 * P:3 * P], KTB[:, 3, :], QT[:, 3 * P:SEQ], start=False, stop=False, skip_group_check=True)
                for b in range(NB):
                    ins = pe.matmul(PS[:, 6, 3 * P + DSEQ * b:3 * P + DSEQ * (b + 1)], KTB[:, 5 + b, :],
                                    QT[:, SEQ + DSEQ * b:SEQ + DSEQ * (b + 1)], start=False, stop=False, skip_group_check=True)
                ins.then_inc(s_z, 1)

            def exponents():
                pe.wait_ge(s_spm, h + 1)
                pe.wait_ge(s_sum, h + 1)
                pe.wait_ge(s_t, h + 1)
                kw = dict(start=False, stop=False, skip_group_check=True)
                pe.matmul(PS[:, 4, P:], ones[:], SUM0[:], **kw)
                pe.matmul(PS[:, 5, P:3 * P], ones[:], SUM1[:], **kw)
                pe.matmul(PS[:, 6, P:2 * P], ones[:], SP_[:, 2, 2 * P:3 * P], **kw)
                pe.matmul(PS[:, 6, 3 * P:], ones[:], SP_[:, 1, 3 * P:], **kw)
                for x in range(3):
                    ins = pe.matmul(PS[:, 4 + x, :], tri[:], SP_[:, x, :], start=False, stop=True, skip_group_check=True)
                    ins.then_inc(s_e, 1)

            def values():
                pe.wait_ge(s_wm, h + 1)
                pe.wait_ge(s_w, h * 3 + 3)
                pe.wait_ge(s_vr, h * 48 + 48)
                kw = dict(skip_group_check=True)
                pe.matmul(PS[:, 7, :], VR[:, 0, :], WT[:, 0, :], start=True, stop=False, **kw)
                pe.matmul(PS[:, 7, P:], VR[:, 1, :], WT[:, 1, 0:3 * P], start=False, stop=False, **kw)
                pe.matmul(PS[:, 7, 2 * P:], VR[:, 2, :], WT[:, 2, 0:2 * P], start=False, stop=False, **kw)
                pe.matmul(PS[:, 7, 3 * P:], VR[:, 3, :], WT[:, 2, 2 * P:3 * P], start=False, stop=True, **kw).then_inc(s_o, 1)
                pe.matmul(PS[:, 4, 0:P], VR[:, 4, :], WT[:, 1, 3 * P:], start=True, stop=False, **kw)
                for b in range(NB):
                    c = slice(DSEQ * b, DSEQ * (b + 1))
                    ins = pe.matmul(PS[:, 4, c], VR[:, 5 + b, :], WT[:, 2, 3 * P + DSEQ * b:3 * P + DSEQ * (b + 1)],
                                    start=False, stop=True, **kw)
                ins.then_inc(s_o, 1)

            return turn, scores, exponents, values

        def loop_wait(pool, s, count):
            count = pool.snap(pool.to_reg(count))
            pool.wait_ge(s_memset, 1)
            pool.wait_ge(s, count)

        def sb_pool(pool, mine, i):
            for r in range(2):
                h = i * 2 + r
                loop_wait(pool, s_kt, h * 4 + 4)
                for name, dst, s in (("k", KR, s_kr), ("v", VR, s_vr)):
                    if name == "v":
                        loop_wait(pool, s_o, h * 2 + 2)
                    hd = (slice(None), slice(None), ds(h, 1))
                    a = out[f"{name}_prompt"][0].rearrange("(t p) h d -> h p t d", p=P)[ds(h, 1)].rearrange("o p t d -> (o p) t d")
                    pool.dma_start(dst[:, 0:4, :], a).then_inc(s, 16)
                    a = out[f"{name}_sample"].rearrange("b i h d -> h (b i) d")[ds(h, 1)].rearrange("o p d -> (o p) d")
                    pool.dma_start(dst[:, 4, :], a).then_inc(s, 16)
                    a = io[f"cache_{name}"].rearrange("b p h d -> h p b d")[ds(h, 1)].rearrange("o p b d -> (o p) b d")
                    pool.dma_start(dst[:, 5:13, :], a).then_inc(s, 16)
                for src, ready, done in ((SP_, s_sp, s_spm), (WT, s_w, s_wm)):
                    loop_wait(pool, ready, h * 3 + 3)
                    for x, c in DIAG + [NEW]:
                        v = src[:, x, c:c + P]
                        ins = pool.affine_select(out=v, in_=v, compare_op=ALU.is_gt, fill=0.0, base=0, pattern=[[1, P]], channel_multiplier=-1)
                    mine(ins)
                    loop_wait(pool, mine.sem, mine.count())
                    v = src[:, NEW[0], NEW[1]:NEW[1] + P].rearrange("p (b i) -> p b i", b=NB)
                    pool.affine_select(out=v, in_=v, compare_op=ALU.is_ge, fill=0.0, base=0,
                                       pattern=[[-DSEQ, NB], [0, DSEQ]], channel_multiplier=1).then_inc(done, 1)

        def sb_act(act, i, r):
            h = i * 2 + r

            def turn():
                for m in range(2):
                    act.wait_ge(s_st["in_b"][m], i * 32 + 16)
                act.wait_ge(s_qt, h + 1)
                act.dma_start(QR[:], scr["in_b"][ds(h, 1)].rearrange("o p n -> (o p) n")).then_inc(s_q, 16)
                act.wait_ge(s_z, h + 1)
                for x in range(4):
                    n = min(4, 13 - 4 * x)
                    act.wait_ge(s_kt, h * 4 + 5 + x)
                    act.activation(KTB[:, 4 * x:4 * x + n, :], PS[:, 4 + x, 0:n * P].rearrange("p (j m) -> p j m", m=P), ACT.Copy).then_inc(s_kte, 1)
                act.wait_ge(s_q, h * 16 + 16)
                act.activation(QT[:], QR[:], ACT.Copy, scale=SCALE).then_inc(s_qt, 1)

            def softplus():
                act.wait_ge(s_z, h + 2)
                act.activation(TP[:], PS[:, 4:7, :], ACT.Abs).then_inc(s_ab, 1)
                act.wait_ge(s_ab, h * 2 + 1)
                act.activation(TP[:], TP[:], ACT.Exp, scale=-1.0).then_inc(s_ab, 1)
                act.wait_ge(s_ab, h * 2 + 2)
                act.activation(TP[:], TP[:], ACT.Ln, bias=1.0).then_inc(s_t, 1)

            def exponential():
                act.wait_ge(s_o, h * 2 + 2)
                for x in range(3):
                    act.wait_ge(s_e, h * 3 + 1 + x)
                    act.activation(WT[:, x, :], PS[:, 4 + x, :], ACT.Exp).then_inc(s_w, 1)

            def output():
                act.wait_ge(s_ost, h * 16 + 16)
                act.wait_ge(s_o, h * 2 + 3)
                act.activation(OS[:, 0:SEQ], PS[:, 7, :], ACT.Copy).then_inc(s_oe, 1)
                act.wait_ge(s_o, h * 2 + 4)
                act.activation(OS[:, SEQ:TOK], PS[:, 4, 0:P], ACT.Copy).then_inc(s_oe, 1)
                act.wait_ge(s_oe, h * 2 + 4)
                act.dma_start(scr["out_b"][ds(h, 1)].rearrange("o p n -> (o p) n"), OS[:]).then_inc(s_ost, 16)

            return turn, softplus, exponential, output

        s_ab = sem("magnitudes")

        def sb_dve(dve, mine, i, r):
            h = i * 2 + r

            def softplus():
                dve.wait_ge(s_t, h + 1)
                for x in range(3):
                    dve.scalar_tensor_tensor(out=SP_[:, x, :], in0=PS[:, 4 + x, :], scalar=0.0, in1=TP[:, x, :],
                                             op0=ALU.max, op1=ALU.add).then_inc(s_sp, 1)
                dve.wait_ge(s_spm, h + 1)
                mine(dve.tensor_copy(SUM1[:, 0:P], SP_[:, 2, 0:P]))
                mine(dve.tensor_tensor(SUM1[:, P:], SP_[:, 2, P:2 * P], SP_[:, 2, 2 * P:3 * P], ALU.add))
                mine(dve.tensor_copy(SUM0[:, 0:P], SP_[:, 1, 0:P]))
                mine.wait()
                dve.tensor_tensor(SUM0[:, P:], SP_[:, 1, P:3 * P], SUM1[:], ALU.add).then_inc(s_sum, 1)

            return softplus

        DVE_SSM, POOL_SSM = 67, 11
        block = ctx.enter_context(nc.Block())

        @block.sync
        def _(sp):
            def src_wide(w, k, kts, c0, cw):
                return w.rearrange("(k p) n -> p k n", p=P)[:, k * kts:(k + 1) * kts, c0:c0 + cw] if isinstance(c0, int) \
                    else w.rearrange("(k p) n -> p k n", p=P)[:, k * kts:(k + 1) * kts, ds(c0, cw)]

            for r in range(2):
                sp.dma_start(ROWS_IN[r], io["mem_prompt"][0, P * r:P * r + P, :]).then_inc(s_memd, 16)
            ph = phases["mem"]
            for c in range(4):
                w = (io["w_mem_k"] if c % 2 == 0 else io["w_mem_v"])[c // 2]
                for k in range(ph.upc):
                    load_unit(sp, ph, ph.first + 8 * c + k, k, src_wide(w, k, 2, 0, RW))

            def chunk(ph, n, col):
                for k in range(ph.upc):
                    load_unit(sp, ph, ph.first + ph.upc * n + k, k, src_wide(ph.w, k, ph.kts, col, ph.cw))

            def projections(ph):
                chunk(ph, 0, 0)
                with sp.Fori(0, BATCHES) as i:
                    chunk(ph, 2 * i + 1, i * CW + CW)
                    chunk(ph, 2 * i + 2, i * CW + 10 * CW)
                for n in range(13, 16):
                    chunk(ph, n, (n - 6) * CW)

            def plain(ph):
                with sp.Fori(0, ph.chunks) as i:
                    chunk(ph, i, i * ph.cw)

            projections(phases["in_a"])
            plain(phases["glu"])
            plain(phases["out_a"])
            plain(phases["kv"])
            projections(phases["in_b"])
            plain(phases["out_b"])
        def unit_stationary(pe, ph, U, k, n, between=None):
            pe.wait_ge(s_wl, U + 1)
            pe.wait_ge(s_wh, U + 1)
            wh, wl = wview(WH, k % RING, ph), wview(WL, k % RING, ph)
            for q in range(4):
                m, h = q // 2, q % 2
                if between:
                    between(q)
                if k == 0 and not (isinstance(n, int) and n == 0):
                    pe.wait_ge(s_ev[ph.name], 4 * n - 3 + q)
                for kt in range(ph.kts):
                    last = k == ph.upc - 1 and kt == ph.kts - 1
                    x = (slice(None), k * ph.kts + kt, slice(h * HALF, h * HALF + HALF))
                    w = (slice(None), kt, slice(m * P, m * P + P))
                    ins = three(pe, PS[:, q, 0:HALF], wh[w], wl[w], XH[x], XL[x], k == 0 and kt == 0, last)
                if q == 3:
                    ins.then_inc(s_wu, 1)
                elif k == ph.upc - 1:
                    ins.then_inc(s_bank[ph.name], 1)

        def unit_moving(pe, ph, U, k, n, tiles, fill=None):
            pe.wait_ge(s_wl, U + 1)
            pe.wait_ge(s_wh, U + 1)
            wh, wl = wview(WH, k % RING, ph), wview(WL, k % RING, ph)
            for t in range(tiles):
                if k == 0 and not (isinstance(n, int) and n == 0):
                    pe.wait_ge(s_ev[ph.name], tiles * n - tiles + 1 + t)
                if fill and t == 0:
                    first, order = fill
                    pe.wait_ge(s_fl, first + 1 + max(order.index(k * ph.kts + x) for x in range(ph.kts)))
                for kt in range(ph.kts):
                    xh, xl = XH[:, k * ph.kts + kt, P * t:P * t + P], XL[:, k * ph.kts + kt, P * t:P * t + P]
                    first, last = k == 0 and kt == 0, k == ph.upc - 1 and kt == ph.kts - 1
                    pe.matmul(PS[:, t, :], xh, wh[:, kt, :], start=first, stop=False)
                    pe.matmul(PS[:, t, :], xh, wl[:, kt, :], start=False, stop=False)
                    ins = pe.matmul(PS[:, t, :], xl, wh[:, kt, :], start=False, stop=last)
                if t == tiles - 1:
                    ins.then_inc(s_wu, 1)
                elif k == ph.upc - 1:
                    ins.then_inc(s_bank[ph.name], 1)

        def bank_full(eng, ph, n, q, banks):
            if q == banks - 1:
                eng.wait_ge(s_wu, ph.upc * n + ph.first + ph.upc)
            else:
                eng.wait_ge(s_bank[ph.name], (banks - 1) * n + q + 1)

        def turn_bank(x):
            return 5 + x % 3

        def turn_rows(pe, r, row):
            for kg in range(4):
                x = 4 * r + kg
                if x >= 3:
                    pe.wait_ge(s_xl, x - 2)
                for j in range(4):
                    kt = 4 * kg + j
                    ins = pe.transpose(PS[:, turn_bank(x), j * P:(j + 1) * P], row[:, kt * P:(kt + 1) * P], ident[:])
                ins.then_inc(s_xt, 1)

        def turned_view(v, r, kg):
            v = v[:, 4 * kg:4 * kg + 4, :]
            if r < 2:
                return v[:, :, P * r:P * r + P]
            if r < 7:
                return v.rearrange("p k (s c) -> p k s c", s=STEPS)[:, :, :, 16 * (r - 2):16 * (r - 2) + 16]
            return v[:, :, P * (r - 7):P * (r - 7) + P]

        def bank_view(r, x):
            v = PS[:, turn_bank(x), :].rearrange("p (k m) -> p k m", k=4)
            return v if r < 2 or r >= 7 else v.rearrange("p k (s c) -> p k s c", s=STEPS)

        def turned_high(act, r):
            for kg in range(4):
                x = 4 * r + kg
                act.wait_ge(s_xt, x + 1)
                act.activation(turned_view(XH, r, kg), bank_view(r, x), ACT.Copy).then_inc(s_xh, 1)

        def turned_low(dve, r):
            for kg in range(4):
                x = 4 * r + kg
                dve.wait_ge(s_xh, x + 1)
                dve.tensor_tensor(turned_view(XL, r, kg), bank_view(r, x), turned_view(XH, r, kg).bitcast(F32),
                                  ALU.subtract).then_inc(s_xl, 1)

        def stage_out(act, ph, n, q, banks, stage, width):
            bank_full(act, ph, n, q, banks)
            act.activation(stage, PS[:, q, 0:width], ACT.Copy).then_inc(s_ev[ph.name], 1)

        def rows_squared(act, src, col, done, junk):
            if done:
                act.wait_ge(s_sq, done)
            act.activation(junk, src, ACT.Square, accum_out=ss[:, col:col + 1]).then_inc(s_sq, 1)

        s_yout = sem("y_rows_stored")

        def inverse_rms(pool, order, k, summed, count, n=1):
            pool.wait_ge(summed, count)
            a = slice(k, k + n)
            order(pool.tensor_scalar(rstd[:, a], ss[:, a], 1.0 / D, EPS, ALU.mult, ALU.add))
            order.wait()
            pool.tensor_tensor(rstd[:, a], rstd[:, a], nhalf[:, 0:n], ALU.pow).then_inc(s_rs, n)

        @block.tensor
        def _(pe):
            pe.wait_ge(s_memset, 1)
            pe.wait_ge(s_memd, 32)
            for r in range(2):
                turn_rows(pe, r, ROWS_IN[r])
            pe.wait_ge(s_vecd, 64)
            pe.wait_ge(s_xl, 8)
            pe.transpose(PS[:, 7, 0:60], VROW[0:60, :], ident[0:60, 0:60]).then_inc(s_vect, 1)
            pe.wait_ge(s_par, 64)
            pe.wait_ge(s_parE, 1)
            pe.wait_ge(s_vec, 1)
            for j, (src, n) in enumerate(((PRM[0:48, 0, :], 48), (PRM[0:48, 1, :], 48), (PRM[0:48, 2, :], 48), (PRD[0:G, :], G))):
                ins = pe.transpose(PS[:, 7, 64 + 48 * j:64 + 48 * j + n], src, ident[0:n, 0:n])
            ins.then_inc(s_parT, 1)
            ph = phases["mem"]
            pe.wait_ge(s_xl, 8)
            for n in range(4):
                for k in range(ph.upc):
                    unit_moving(pe, ph, ph.first + 8 * n + k, k, n, 2)
            pe.wait_ge(s_pw, 1)
            for t in range(NT):
                pe.wait_ge(s_row, t + 1)
                turn_rows(pe, t + 2, ROWS_IN[(t + 2) % 4])
            ph = phases["in_a"]
            pe.wait_ge(s_xl, 28)
            pe.wait_ge(s_ev["mem"], 8)

            def chunk(ph, n):
                for k in range(ph.upc):
                    unit_stationary(pe, ph, ph.upc * n + ph.first + k, k, n)

            chunk(ph, 0)
            with pe.Fori(0, BATCHES) as i:
                ssm_pe(pe, ph, i)

            def chunks_with_memory(ph, l):
                for n in range(13, 16):
                    for k in range(ph.upc):
                        at = ((n - 13) * 3 + k) * 4
                        unit_stationary(pe, ph, ph.upc * n + ph.first + k, k, n, (lambda q: mem_pe(pe, l, at + q)) if k < 3 else None)

            pe.wait_ge(s_ye, 21)
            pe.wait_ge(s_fTe, 7)
            chunks_with_memory(ph, 0)
            pe.wait_ge(s_ev["in_a"], 64)
            ph = phases["glu"]
            pe.wait_ge(s_fl, F_Y + MIXB)
            chunk(ph, 0)
            with pe.Fori(1, ph.chunks) as i:
                chunk(ph, i)

            def row_chunks(ph, fill=None):
                for k in range(ph.upc):
                    unit_moving(pe, ph, ph.first + k, k, 0, NT, fill)
                with pe.Fori(1, ph.chunks) as i:
                    for k in range(ph.upc):
                        unit_moving(pe, ph, ph.upc * i + ph.first + k, k, i, NT)

            pe.wait_ge(s_ev["glu"], 24)
            row_chunks(phases["out_a"], (F_A, ORDER_A))
            pe.wait_ge(s_ev["out_a"], 20)
            for t in range(NT):
                pe.wait_ge(s_row, NT + t + 1)
                turn_rows(pe, 7 + t, RES[t % 3])
            pe.wait_ge(s_xl, 48)
            row_chunks(phases["kv"])
            pe.wait_ge(s_ev["kv"], 30)
            ph = phases["in_b"]
            chunk(ph, 0)
            with pe.Fori(0, BATCHES) as i:
                first, second = sb_pe(pe, i, 0), sb_pe(pe, i, 1)
                plan = {0: [first[0]], 1: [first[1]], 3: [first[2]], 4: [first[3], second[0]], 5: [second[1]], 7: [second[2]]}
                for x in range(8):
                    for f in plan.get(x, ()):
                        f()
                    n = i * 2 + 1 + x // 4
                    unit_stationary(pe, ph, (i * 2 + 1 + x // 4) * 4 + ph.first + x % 4, x % 4, n)
                second[3]()
            pe.wait_ge(s_oe, 26)
            chunks_with_memory(ph, 1)
            pe.wait_ge(s_ev["in_b"], 64)
            row_chunks(phases["out_b"], (F_B, ORDER_B))

        @block.scalar
        def _(act):
            mine = Order(act, s_act)
            for r in range(2):
                turned_high(act, r)
            for U in range(LEAD):
                split_high(act, phases["mem"], U, U)
            act.wait_ge(s_vect, 1)
            act.activation(vec[:, 0:60], PS[:, 7, 0:60], ACT.Copy).then_inc(s_vec, 1)
            act.wait_ge(s_vec, 1)
            ph = phases["mem"]
            for n in range(4):
                for k in range(ph.upc):
                    ahead(split_high, act, ph, ph.first + ph.upc * n + k, k)
                for t in range(2):
                    if n:
                        act.wait_ge(s_st["mem"][t], 16 * n)
                    stage_out(act, ph, n, t, 2, EST[:, t, 0:RW], RW)
                    act.wait_ge(s_ev["mem"], 2 * n + t + 1)
                    dst = out["mem_k_prompt" if n % 2 == 0 else "mem_v_prompt"][n // 2, 0].rearrange("m h d -> m (h d)")
                    act.dma_start(dst[P * t:P * t + P, :], EST[:, t, 0:RW]).then_inc(s_st["mem"][t], 16)
                if n < 2:
                    for t in (2 * n, 2 * n + 1):
                        act.wait_ge(s_rowd[(t + 2) % 4], 16)
                        rows_squared(act, ROWS_IN[(t + 2) % 4], t, t, JUNK[:])
                if n == 0:
                    act.wait_ge(s_trig, 1)
                    act.activation(CPT(11), CPT(8), ACT.Sin)
                    act.activation(CPT(12), CPT(10), ACT.Sin).then_inc(s_sin, 1)
            for t in range(NT):
                turned_high(act, t + 2)
                if t == 1:
                    act.wait_ge(s_rowd[2], 32)
                    rows_squared(act, ROWS_IN[2], 4, 4, JUNK[:])
            ph = phases["in_a"]

            def store_blocks(name, n, col, q):
                m, h = q // 2, q % 2
                ph = phases[name]
                if h == 0:
                    if not (isinstance(n, int) and n == 0):
                        act.wait_ge(s_st[name][m], n * 16)
                bank_full(act, ph, n, q, 4)
                act.activation(EST[:, m, h * HALF:h * HALF + HALF], PS[:, q, 0:HALF], ACT.Copy).then_inc(s_ev[name], 1)
                if h == 1:
                    act.wait_ge(s_ev[name], n * 4 + q + 1)
                    dst = scr[name][ds(col * 2 + m, 1)].rearrange("o p n -> (o p) n") if not isinstance(col, int) \
                        else scr[name][col * 2 + m]
                    act.dma_start(dst, EST[:, m, :]).then_inc(s_st[name][m], 16)

            def chunk(name, n, col, aux=()):
                ph = phases[name]
                for k in range(ph.upc):
                    ahead(split_high, act, ph, ph.upc * n + ph.first + k, k)
                    if k < len(aux) and aux[k]:
                        aux[k]()
                for q in range(4):
                    store_blocks(name, n, col, q)

            for t in range(2):
                act.wait_ge(s_st["mem"][t], 64)
            chunk("in_a", 0, 0)
            with act.Fori(0, BATCHES) as i:
                aux = ssm_act(act, mine, i)
                chunk("in_a", i * 2 + 1, i + 1, aux[0:4])
                chunk("in_a", i * 2 + 2, i + 10, aux[4:8])
                aux[8]()
            ph = phases["in_a"]
            for n in range(13, 16):
                for k in range(ph.upc):
                    U = ph.upc * n + ph.first + k
                    ahead(split_high, act, ph, U, k)
                    if k < 3:
                        mem_act(act, 0, (n - 13) * 3 + k)
                        if n == 13 and k == 1:
                            mem_gates_act(act, 0)
                    else:
                        act.wait_ge(s_am[n - 13], 16)
                        for kb in range(4 * (n - 13), 4 * (n - 13) + 4):
                            act.activation(AM[:, kb, :], AM[:, kb, :], ACT.Gelu_apprx_tanh).then_inc(s_gel, 1)
                    if n == 15 and k:
                        act.wait_ge(s_wu, U)
                        for kb in range(4 * k - 4, 4 * k):
                            act.wait_ge(s_gel, kb + 1)
                            fill_high(act, F_Y, kb)
                for q in range(4):
                    store_blocks("in_a", n, n - 6, q)
            ph = phases["glu"]
            for n in range(ph.chunks):
                for k in range(ph.upc):
                    ahead(split_high, act, ph, ph.upc * n + ph.first + k, k)
                    if n == 0 and k == 0:
                        layer_wait(act, 0, "gated", NT)
                        act.wait_ge(s_wu, ph.first)
                        for kb in range(MIXB, KT):
                            fill_high(act, F_A, kb)
                    if n == ph.chunks - 1 and k:
                        act.wait_ge(s_wu, ph.upc * n + ph.first + k)
                        for kb in range(3 * k - 3, 3 * k):
                            act.wait_ge(s_gm, kb + 1)
                            fill_high(act, F_A, kb)
                    if k < 2:
                        kb = 2 * n + k
                        act.wait_ge(s_gt[k], 16 * (n + 1))
                        if kb >= 2:
                            act.wait_ge(s_gm, kb - 1)
                        act.activation(GS[:, k, :], GT[:, k, :], ACT.Sigmoid).then_inc(s_gs, 1)
                for q in range(4):
                    m, h = q // 2, q % 2
                    if n and h == 0:
                        act.wait_ge(s_gm, 2 * n - 1 + m)
                    bank_full(act, ph, n, q, 4)
                    act.activation(SG[:, m, h * HALF:h * HALF + HALF], PS[:, q, 0:HALF], ACT.Sigmoid,
                                   bias=vec[:, 48 + 2 * n + m:49 + 2 * n + m]).then_inc(s_ev["glu"], 1)
            for kb in range(9, MIXB):
                act.wait_ge(s_gm, kb + 1)
                fill_high(act, F_A, kb)

            def out_rows_squared(l):
                ph = phases[DST[l]]
                for n in range(ph.chunks):
                    for k in range(ph.upc):
                        ahead(split_high, act, ph, ph.upc * n + ph.first + k, k)
                    for t in range(NT):
                        bank_full(act, ph, n, t, NT)
                        if n or t:
                            act.wait_ge(s_osq[l], NT * n + t)
                        act.activation(JUNK2[:], PS[:, t, :], ACT.Square, accum_out=ss4[:, l, t, n:n + 1]).then_inc(s_osq[l], 1)

            out_rows_squared(0)

            def x1_squared(t):
                act.wait_ge(s_x1, t + 1)
                rows_squared(act, OUTROW[:, t, :], 10 + t, NT + t, RES[t % 3])

            x1_squared(0)
            x1_squared(1)
            for t in range(NT):
                turned_high(act, 7 + t)
                if t + 2 < NT:
                    x1_squared(t + 2)
            ph = phases["kv"]

            def kv_chunk(n, name, col):
                for k in range(ph.upc):
                    ahead(split_high, act, ph, ph.upc * n + ph.first + k, k)
                for t in range(NT):
                    if not (isinstance(n, int) and n == 0):
                        act.wait_ge(s_kvst[t], n * 16)
                    bank_full(act, ph, n, t, NT)
                    act.activation(KV_STAGE[:, t, :], PS[:, t, :], ACT.Copy).then_inc(s_ev["kv"], 1)
                for t in range(NT):
                    act.wait_ge(s_ev["kv"], n * NT + t + 1)
                    dst = out[f"{name}_prompt"][0].rearrange("l h d -> l (h d)")[P * t:P * t + P] if t < NT - 1 else \
                        out[f"{name}_sample"].rearrange("b i h d -> (b i) (h d)")
                    act.dma_start(dst[:, ds(col, RW)], KV_STAGE[:, t, :]).then_inc(s_kvst[t], 16)

            kv_chunk(0, "k", 0)
            with act.Fori(1, 3) as i:
                kv_chunk(i, "k", i * RW)
            with act.Fori(3, 5) as i:
                kv_chunk(i, "v", i * RW - 3 * RW)
            kv_chunk(5, "v", 2 * RW)
            chunk("in_b", 0, 0)
            with act.Fori(0, BATCHES) as i:
                first, second = sb_act(act, i, 0), sb_act(act, i, 1)

                def between():
                    first[3]()
                    second[0]()

                chunk("in_b", i * 2 + 1, i + 1, [first[0], first[1], None, first[2]])
                chunk("in_b", i * 2 + 2, i + 10, [between, second[1], None, second[2]])
                second[3]()
            ph = phases["in_b"]
            def load_gate(j):
                act.dma_start(GB1[:], scr["in_b"][MIXB + GATE_BLOCKS[j]]).then_inc(s_gb_ld, 16)

            for m in range(2):
                act.wait_ge(s_st["in_b"][m], 208)
            for n in range(13, 16):
                for k in range(ph.upc):
                    U = ph.upc * n + ph.first + k
                    ahead(split_high, act, ph, U, k)
                    if k < 3:
                        mem_act(act, 1, (n - 13) * 3 + k)
                        if n == 13 and k == 1:
                            mem_gates_act(act, 1)
                            layer_wait(act, 1, "gate_ready", MH)
                            load_gate(0)
                        j = (n - 13) * 3 + k - 2
                        if 0 <= j < 6:
                            act.wait_ge(s_gd, j + 1)
                            act.activation(GB1[:], GB1[:], ACT.Sigmoid).then_inc(s_gd1, 1)
                            act.wait_ge(s_gd2, j + 1)
                            if j < 5:
                                load_gate(j + 1)
                    if n == 15 and k:
                        act.wait_ge(s_wu, U)
                        for x in ORDER_B[0:4] if k == 1 else ORDER_B[4:6] if k == 2 else ORDER_B[6:10]:
                            fill_high(act, F_B, x)
                for q in range(4):
                    m, h = q // 2, slice(q % 2 * HALF, q % 2 * HALF + HALF)
                    bank_full(act, ph, n, q, 4)
                    if n > 13:
                        act.wait_ge(s_gq, 4 * (n - 14) + q + 1)
                    act.activation(EST[:, m, h], PS[:, q, 0:HALF], ACT.Sigmoid).then_inc(s_gsq, 1)
            act.wait_ge(s_gq, 12)
            layer_wait(act, 1, "gated", NT)
            act.wait_ge(s_wu, phases["out_b"].first)
            for x in ORDER_B[10:]:
                fill_high(act, F_B, x)
            out_rows_squared(1)

        @block.vector
        def _(dve):
            mine = Order(dve, s_dve)
            for r in range(2):
                turned_low(dve, r)
            for U in range(LEAD):
                split_low(dve, phases["mem"], U, U)
            ssm_params(dve, mine)
            dve.wait_ge(s_vec, 1)
            ssm_params2(dve, mine)

            def row_normalised(t):
                dve.wait_ge(s_rs, t + 1)
                row = ROWS_IN[(t + 2) % 4]
                dve.tensor_scalar(row, row, rstd[:, t:t + 1], None, ALU.mult).then_inc(s_row, 1)

            ph = phases["mem"]
            for n in range(4):
                for k in range(ph.upc):
                    ahead(split_low, dve, ph, ph.first + ph.upc * n + k, k)
                if n == 0:
                    ssm_params3(dve, mine)
                if n == 2:
                    for t in range(NT - 1):
                        row_normalised(t)
            for t in range(NT):
                turned_low(dve, t + 2)
                if t == 1:
                    row_normalised(NT - 1)

            def chunk(ph, n, aux=()):
                for k in range(ph.upc):
                    ahead(split_low, dve, ph, ph.upc * n + ph.first + k, k)
                    if k < len(aux) and aux[k]:
                        aux[k]()

            ph = phases["in_a"]
            chunk(ph, 0)
            with dve.Fori(0, BATCHES) as i:
                mine.enter(i, DVE_SSM)
                aux = ssm_dve(dve, mine, i)
                chunk(ph, i * 2 + 1, aux[0:4])
                chunk(ph, i * 2 + 2, aux[4:8])
                aux[8]()
                mine.leave(BATCHES)
            for n in range(13, 16):
                for k in range(ph.upc):
                    ahead(split_low, dve, ph, ph.upc * n + ph.first + k, k)
                    if n == 13 and k == 0:
                        mem_queries_dve(dve, 0)
                    if k < 3:
                        mem_dve(dve, mine, 0, (n - 13) * 3 + k)
                    if n == 13 and k == 1:
                        mem_gates_dve(dve, 0)
                    if n == 15 and k:
                        for kb in range(4 * k - 4, 4 * k):
                            fill_low(dve, F_Y, kb, kb)
            ph = phases["glu"]
            for n in range(ph.chunks):
                for k in range(ph.upc):
                    ahead(split_low, dve, ph, ph.upc * n + ph.first + k, k)
                    if n == 0 and k == 0:
                        for x in range(4):
                            fill_low(dve, F_A, x, ORDER_A[x])
                    if n == ph.chunks - 1 and k:
                        for kb in range(3 * k - 3, 3 * k):
                            fill_low(dve, F_A, 4 + kb, kb)
                for m in range(2):
                    kb = 2 * n + m
                    dve.wait_ge(s_gs, kb + 1)
                    mine(dve.tensor_tensor(GS[:, m, :], GS[:, m, :], GT[:, m, :], ALU.mult))
                    mine.wait()
                    mine(dve.tensor_tensor(AM[:, kb, :], AM[:, kb, :], GS[:, m, :], ALU.mult))
                    mine.wait()
                    dve.wait_ge(s_ev["glu"], 4 * n + 2 * m + 2)
                    dve.tensor_tensor(AM[:, kb, :], AM[:, kb, :], SG[:, m, :], ALU.mult).then_inc(s_gm, 1)
            for kb in range(9, MIXB):
                fill_low(dve, F_A, 4 + kb, kb)

            def out_rows(l):
                ph = phases[DST[l]]
                for n in range(ph.chunks):
                    for k in range(ph.upc):
                        ahead(split_low, dve, ph, ph.upc * n + ph.first + k, k)
                    if n == 0:
                        dve.wait_ge(s_gb, 16 * (l + 1))
                    for t in range(NT):
                        dve.wait_ge(s_osq[l], NT * n + t + 1)
                        c = slice(n * RW, n * RW + RW)
                        dve.tensor_tensor(OUTROW[:, t, c], PS[:, t, :], GB[:, c], ALU.mult).then_inc(s_ev[ph.name], 1)
                k = NT + 2 * NT * l
                dve.tensor_reduce(ss[:, k:k + NT], ss4[:, l], AX.X, ALU.add).then_inc(s_osum, 1)

            def residual(l, t):
                v = NT * l + t
                dve.wait_ge(s_rs, 5 + 10 * l + t + 1)
                dve.wait_ge(s_resd[v % 3], 16 * (v // 3 + 1))
                dve.wait_ge(s_ev[DST[l]], 20)
                k = 5 + 10 * l + t
                dve.scalar_tensor_tensor(out=OUTROW[:, t, :], in0=OUTROW[:, t, :], scalar=rstd[:, k:k + 1], in1=RES[v % 3],
                                         op0=ALU.mult, op1=ALU.add).then_inc(s_x1, 1)

            out_rows(0)
            residual(0, 0)
            residual(0, 1)
            for t in range(NT):
                dve.wait_ge(s_rs, 10 + t + 1)
                dve.tensor_scalar(RES[t % 3], OUTROW[:, t, :], rstd[:, 10 + t:11 + t], None, ALU.mult).then_inc(s_row, 1)
                turned_low(dve, 7 + t)
                if t + 2 < NT:
                    residual(0, t + 2)
            ph = phases["kv"]
            with dve.Fori(0, 5) as i:
                chunk(ph, i)
            chunk(ph, 5)
            ph = phases["in_b"]
            chunk(ph, 0)
            with dve.Fori(0, BATCHES) as i:
                mine.enter(i, 6)
                chunk(ph, i * 2 + 1, [None, sb_dve(dve, mine, i, 0)])
                chunk(ph, i * 2 + 2, [None, sb_dve(dve, mine, i, 1)])
                mine.leave(BATCHES)
            for n in range(13, 16):
                for k in range(ph.upc):
                    ahead(split_low, dve, ph, ph.upc * n + ph.first + k, k)
                    if n == 13 and k == 0:
                        mem_queries_dve(dve, 1)
                    if k < 3:
                        mem_dve(dve, mine, 1, (n - 13) * 3 + k)
                        if n == 13 and k == 1:
                            mem_gates_dve(dve, 1)
                        j = (n - 13) * 3 + k - 2
                        if j == 0:
                            for x in range(2):
                                dve.wait_ge(s_am[x], 32)
                        if 0 <= j < 6:
                            kb = GATE_BLOCKS[j]
                            dve.wait_ge(s_gb_ld, 16 * (j + 1))
                            dve.tensor_tensor(AM[:, kb, :], AM[:, kb, :], GB1[:], ALU.mult).then_inc(s_gd, 1)
                            dve.wait_ge(s_gd1, j + 1)
                            dve.wait_ge(s_gd, j + 1)
                            dve.tensor_tensor(AM[:, kb, :], AM[:, kb, :], GB1[:], ALU.mult).then_inc(s_gd2, 1)
                    if n == 15 and k:
                        for x in range(4) if k == 1 else range(4, 6) if k == 2 else range(6, 10):
                            fill_low(dve, F_B, x, ORDER_B[x])
                for q in range(4):
                    m, h, kb = q // 2, slice(q % 2 * HALF, q % 2 * HALF + HALF), 2 * (n - 12) + q // 2
                    dve.wait_ge(s_gsq, 4 * (n - 13) + q + 1)
                    dve.tensor_tensor(EST[:, m, h], PS[:, q, 0:HALF], EST[:, m, h], ALU.mult).then_inc(s_ev["in_b"], 1)
                    dve.wait_ge(s_ev["in_b"], 4 * n + q + 1)
                    dve.tensor_tensor(AM[:, kb, h], AM[:, kb, h], EST[:, m, h], ALU.mult).then_inc(s_gq, 1)
            for x in range(10, KT):
                fill_low(dve, F_B, x, ORDER_B[x])
            out_rows(1)
            for t in range(NT):
                residual(1, t)

        @block.gpsimd
        def _(pool):
            mine = Order(pool, s_pool)
            mine(pool.memset(ident[:], 0.0))
            mine(pool.memset(nhalf[:], -0.5))
            mine(pool.memset(tri[:], -1.0))
            mine(pool.memset(ones[:], -1.0))
            mine.wait()
            mine(pool.affine_select(out=ident[:], in_=ident[:], compare_op=ALU.not_equal, fill=1.0, base=0,
                                    pattern=[[-1, P]], channel_multiplier=1))
            mine(pool.affine_select(out=tri[:], in_=tri[:], compare_op=ALU.is_ge, fill=0.0, base=0,
                                    pattern=[[-1, P]], channel_multiplier=1))
            mine.wait()
            pool.memset(marks[0:1, 0:1], 0.0).then_inc(s_memset, 1)
            for a, b, name in ((0, 16, "g_pre_a"), (16, 32, "g_kv"), (32, 48, "g_pre_b"), (48, 60, "b_glu")):
                v = io[name] if name == "g_kv" else io[name][0]
                pool.dma_start(VROW[a:b, :], v.rearrange("(k p) -> k p", p=P)).then_inc(s_vecd, 16)
            for j, name in enumerate(("ssm_lam_re", "ssm_lam_im")):
                pool.dma_start(PRM[0:48, j, :], io[name][0].rearrange("(j q) p -> j (q p)", q=2)).then_inc(s_par, 16)
            pool.dma_start(PRL[0:48, :], io["ssm_log_dt"][0].rearrange("(j q) -> j q", q=2)).then_inc(s_par, 16)
            pool.dma_start(DRW[0:G, :], io["ssm_d"][0]).then_inc(s_par, 16)
            pool.memset(BB[:], 0.0).then_inc(s_zero, 1)
            prime_ssm(pool)
            for k, (s, n) in enumerate(((s_oe, 2), (s_kt, 4), (s_qt, 1), (s_z, 1), (s_o, 2), (s_ost, 16))):
                pool.memset(marks[0:1, 20 + k:21 + k], 0.0).then_inc(s, n)
            for t, used in enumerate((1, 3, 8, 11)):
                pool.wait_ge(s_wu, used)
                pool.dma_start(ROWS_IN[(t + 2) % 4], x_rows(t)).then_inc(s_rowd[(t + 2) % 4], 16)
            ssm_params_pool(pool, mine)
            for t in range(NT):
                if t == NT - 1:
                    pool.wait_ge(s_xt, 12)
                    pool.dma_start(ROWS_IN[2], x_rows(t)).then_inc(s_rowd[2], 16)
                inverse_rms(pool, mine, t, s_sq, t + 1)
            pool.wait_ge(s_xt, 4 * (NT + 2))
            pool.memset(TZ[:], 0.0).then_inc(s_zero, 1)
            pool.memset(HPZ[:], 0.0).then_inc(s_zero, 1)
            with pool.Fori(0, BATCHES) as i:
                mine.enter(i, POOL_SSM)
                ssm_pool(pool, mine, i)
                mine.leave(BATCHES)
            for m in range(2):
                pool.wait_ge(s_st["in_a"][m], 208)
            pool.wait_ge(s_yst, 896)
            pool.wait_ge(s_fst, 224)

            def load_y():
                y = scr["y"].rearrange("(k g) h n -> k (g h) n", k=MIXB)
                for k in range(3):
                    pool.dma_start(AM[:, 4 * k:4 * k + 4, :], y[4 * k:4 * k + 4].rearrange("k p n -> p k n")).then_inc(s_am[k], 16)

            mem_pool(pool, 0, load_y)
            layer_wait(pool, 0, "gated", NT)
            for m in range(2):
                pool.wait_ge(s_st["in_a"][m], 256)
            for kb in range(MIXB):
                if kb >= 2:
                    pool.wait_ge(s_gm, kb - 1)
                pool.dma_start(GT[:, kb % 2, :], scr["in_a"][MIXB + kb]).then_inc(s_gt[kb % 2], 16)
            pool.wait_ge(s_fl, F_B)
            pool.dma_start(GB[:], io["g_post_a"].broadcast_to([P, D])).then_inc(s_gb, 16)
            for t in range(3):
                pool.dma_start(RES[t], x_rows_plain(t)).then_inc(s_resd[t], 16)
            inverse_rms(pool, mine, NT, s_osum, 1, NT)
            for t in range(NT):
                pool.wait_ge(s_x1, t + 1)
                pool.dma_start(scr["x1"][P * t:P * t + P, :], OUTROW[:, t, :]).then_inc(s_x1st, 16)
                inverse_rms(pool, mine, 10 + t, s_sq, NT + t + 1)
                if t + 3 < NT:
                    pool.wait_ge(s_xt, 4 * (8 + t))
                    pool.dma_start(RES[t], x_rows_plain(t + 3)).then_inc(s_resd[t], 16)
            pool.wait_ge(s_x1st, 80)
            for t in range(NT):
                pool.wait_ge(s_kvst[t], 96)
            with pool.Fori(0, BATCHES) as i:
                mine.enter(i, 4)
                sb_pool(pool, mine, i)
                mine.leave(BATCHES)
            for m in range(2):
                pool.wait_ge(s_st["in_b"][m], 208)
            pool.wait_ge(s_ost, 16 * 13)

            def load_heads():
                for k in range(2):
                    pool.dma_start(AM[:, 6 * k:6 * k + 6, :], scr["out_b"][6 * k:6 * k + 6].rearrange("k p n -> p k n")).then_inc(s_am[k], 16)

            mem_pool(pool, 1, load_heads)
            pool.wait_ge(s_fl, F_B + KT)
            pool.dma_start(GB[:], io["g_post_b"].broadcast_to([P, D])).then_inc(s_gb, 16)
            for t in range(3):
                v = NT + t
                pool.dma_start(RES[v % 3], scr["x1"][P * t:P * t + P, :]).then_inc(s_resd[v % 3], 16)
            inverse_rms(pool, mine, 3 * NT, s_osum, 2, NT)
            for t in range(NT):
                pool.wait_ge(s_x1, NT + t + 1)
                if t + 3 < NT:
                    v = NT + t
                    pool.dma_start(RES[v % 3], scr["x1"][P * (t + 3):P * (t + 4), :]).then_inc(s_resd[v % 3], 16)
                dst = out["y_prompt"][0, P * t:P * t + P, :] if t < NT - 1 else out["y_sample"].rearrange("b i d -> (b i) d")
                pool.dma_start(dst, OUTROW[:, t, :]).then_inc(s_yout, 16)
            pool.wait_ge(s_yout, 16 * NT)


_OUTS = [("y_prompt", (1, SEQ, D)), ("y_sample", (NB, DSEQ, D)), ("k_prompt", (1, SEQ, HEADS, P)), ("v_prompt", (1, SEQ, HEADS, P)),
         ("k_sample", (NB, DSEQ, HEADS, P)), ("v_sample", (NB, DSEQ, HEADS, P)), ("ssm_prompt", (1, 1, G, ST, 2)),
         ("ssm_sample", (1, NB, G, ST, 2)), ("mem_k_prompt", (2, 1, NM, MH, P)), ("mem_v_prompt", (2, 1, NM, MH, P))]
_SCRATCH = [("in_a", (NBLK, P, TOK)), ("in_b", (NBLK, P, TOK)), ("y", (G, GH, TOK)), ("lags", (G, GH, P)),
            ("out_a", (KT, P, TOK)), ("out_b", (KT, P, TOK)), ("x1", (TOK, D))]


def kernel(**inputs):
    import numpy as _np
    import concourse.bacc as _bacc
    from concourse import mybir as _mybir
    from concourse.bass_utils import run_bass_kernel_spmd as _run

    nc = _bacc.Bacc("TRN2", target_bir_lowering=False, num_devices=1)
    arrays, io = {}, {}
    for name in inputs:
        a = _np.ascontiguousarray(inputs[name])
        arrays[f"in_{name}_dram"] = a
        io[name] = nc.dram_tensor(f"in_{name}_dram", a.shape, _mybir.dt.from_np(a.dtype), kind="ExternalInput").ap()
    out = {name: nc.dram_tensor(f"out_{name}", shape, F32, kind="ExternalOutput").ap() for name, shape in _OUTS}
    scr = {name: nc.dram_tensor(f"scratch_{name}", shape, F32, kind="Internal").ap() for name, shape in _SCRATCH}
    build(nc, io, out, scr)
    r = _run(nc, [arrays], core_ids=[0])
    return tuple(r.results[0][f"out_{name}"] for name, _ in _OUTS)
```
